# Optimizing a Trainium2 kernel written in Bass

```python
import jax, jax.numpy as jnp
from jax import lax
import numpy as np

D_MODEL = 1024
BATCH = 1
SEQ = 512
DEPTH = 2

MEM_LEN = 256
HEAD_DIM = 64
N_SB_HEADS = 12
N_MEM_HEADS = 4
DIL_GROUPS = ((128, 1), (512, 4), (2048, 16))
HEADS_PER_GROUP = 4
N_DIL_HEADS = HEADS_PER_GROUP * len(DIL_GROUPS)
SB_WIDTH = N_SB_HEADS * HEAD_DIM
MEM_WIDTH = N_MEM_HEADS * HEAD_DIM
DIL_WIDTH = N_DIL_HEADS * HEAD_DIM
D_FF = 2816
CONV_WIDTH = 3
Q_BLOCK = 128
N_A_LAYERS = DEPTH // 2
N_B_LAYERS = DEPTH - N_A_LAYERS
EPS = 1e-6
ALIBI_MAX_BIAS = 8.0

kernel_name = "yoco_stickbreaking_dilated_hybrid"

def rmsnorm(x, g):
    xf = x.astype(jnp.float32)
    y = xf * lax.rsqrt(jnp.mean(xf * xf, axis=-1, keepdims=True) + EPS)
    return (y * g.astype(jnp.float32)).astype(x.dtype)

def alibi_slopes(n):
    return 2.0 ** (-ALIBI_MAX_BIAS * jnp.arange(1, n + 1, dtype=jnp.float32) / n)

def _heads(t, n_heads):
    return t.reshape(t.shape[0], t.shape[1], n_heads, HEAD_DIM)

def stick_breaking_attention(q, k, v):
    s_len = q.shape[1]
    scale = HEAD_DIM ** -0.5
    outs = []
    for blk in range(s_len // Q_BLOCK):
        q0 = blk * Q_BLOCK
        k_end = q0 + Q_BLOCK
        z = jnp.einsum('bqhd,bkhd->bhqk', q[:, q0:k_end], k[:, :k_end]).astype(jnp.float32) * scale
        t_pos = q0 + jnp.arange(Q_BLOCK)[:, None]
        s_pos = jnp.arange(k_end)[None, :]
        causal = s_pos < t_pos
        log_stay = jnp.where(causal, -jax.nn.softplus(z), 0.0)
        later = lax.cumsum(log_stay, axis=3, reverse=True) - log_stay
        w = jnp.where(causal, jnp.exp(jax.nn.log_sigmoid(z) + later), 0.0)
        outs.append(jnp.einsum('bhqk,bkhd->bqhd', w.astype(v.dtype), v[:, :k_end]))
    return jnp.concatenate(outs, axis=1)

def dilated_window_attention(q, k, v, slopes, window, dilation):
    b, s_len, n_h, dh = q.shape
    w_sub = window // dilation
    blk = w_sub
    L = s_len // dilation
    nb = -(-L // blk)
    Lp = nb * blk

    def by_residue(t):
        return t.reshape(b, L, dilation, n_h, dh).transpose(0, 2, 1, 3, 4)

    qs, ks, vs = by_residue(q), by_residue(k), by_residue(v)
    qb = jnp.pad(qs, ((0, 0), (0, 0), (0, Lp - L), (0, 0), (0, 0))).reshape(b, dilation, nb, blk, n_h, dh)

    def key_blocks(t):
        tp = jnp.pad(t, ((0, 0), (0, 0), (blk, Lp - L), (0, 0), (0, 0)))
        prev = tp[:, :, :Lp].reshape(b, dilation, nb, blk, n_h, dh)
        cur = tp[:, :, blk:].reshape(b, dilation, nb, blk, n_h, dh)
        return jnp.concatenate([prev, cur], axis=3)

    kb, vb = key_blocks(ks), key_blocks(vs)
    sc = jnp.einsum('brnqhd,brnkhd->brnhqk', qb, kb).astype(jnp.float32) * dh ** -0.5
    n_idx = jnp.arange(nb)[:, None, None]
    i_idx = jnp.arange(blk)[None, :, None]
    j_idx = jnp.arange(2 * blk)[None, None, :]
    delta = i_idx + blk - j_idx
    valid = (delta >= 0) & (delta <= w_sub) & (n_idx * blk - blk + j_idx >= 0)
    bias = -slopes[None, :, None, None] * (delta * dilation).astype(jnp.float32)[:, None]
    sc = jnp.where(valid[:, None], sc + bias, -jnp.inf)
    m = jnp.max(sc, axis=-1, keepdims=True)
    p = jnp.exp(sc - m)
    denom = jnp.sum(p, axis=-1)
    o = jnp.einsum('brnhqk,brnkhd->brnqhd', p.astype(v.dtype), vb).astype(jnp.float32)
    o = o / jnp.moveaxis(denom, 3, 4)[..., None]
    lse = jnp.moveaxis(m[..., 0] + jnp.log(denom), 3, 4)

    def back(t):
        t = t.reshape((b, dilation, Lp) + t.shape[4:])[:, :, :L]
        t = jnp.swapaxes(t, 1, 2)
        return t.reshape((b, s_len) + t.shape[3:])

    return back(o).astype(q.dtype), back(lse)

def memory_branch(q_mem, mem, norm_mem, w_mem_kv):
    k_m, v_m = jnp.split(rmsnorm(mem, norm_mem) @ w_mem_kv, 2, axis=-1)
    q, k, v = _heads(q_mem, N_MEM_HEADS), _heads(k_m, N_MEM_HEADS), _heads(v_m, N_MEM_HEADS)
    sc = jnp.einsum('bqhd,bkhd->bhqk', q, k).astype(jnp.float32) * HEAD_DIM ** -0.5
    p = jax.nn.softmax(sc, axis=-1)
    o = jnp.einsum('bhqk,bkhd->bqhd', p.astype(v.dtype), v)
    return o.reshape(q_mem.shape)

def conv_ffn(x, w_up, w_conv, w_down):
    s_len = x.shape[1]
    u = x @ w_up
    up = jnp.pad(u, ((0, 0), (CONV_WIDTH - 1, 0), (0, 0)))
    c = w_conv[0] * up[:, 0:s_len]
    for j in range(1, CONV_WIDTH):
        c = c + w_conv[j] * up[:, j:j + s_len]
    a, g = jnp.split(c, 2, axis=-1)
    return (jax.nn.silu(g) * a) @ w_down

def self_decoder_layer(x, mem, norm_attn, w_in, w_out, norm_mem, w_mem_kv, norm_ffn, ffn_up, ffn_conv, ffn_down):
    b, s_len, _ = x.shape
    proj = rmsnorm(x, norm_attn) @ w_in
    q_sb, k_sb, v_sb, q_mem = jnp.split(proj, [SB_WIDTH, 2 * SB_WIDTH, 3 * SB_WIDTH], axis=-1)
    o_sb = stick_breaking_attention(_heads(q_sb, N_SB_HEADS), _heads(k_sb, N_SB_HEADS), _heads(v_sb, N_SB_HEADS))
    o_mem = memory_branch(q_mem, mem, norm_mem, w_mem_kv)
    x = x + jnp.concatenate([o_sb.reshape(b, s_len, SB_WIDTH), o_mem], axis=-1) @ w_out
    return x + conv_ffn(rmsnorm(x, norm_ffn), ffn_up, ffn_conv, ffn_down)

def cross_decoder_layer(x, k_sh, v_sh, mem, norm_attn, w_in, w_out, norm_mem, w_mem_kv, norm_ffn, ffn_up, ffn_conv, ffn_down):
    b, s_len, _ = x.shape
    proj = rmsnorm(x, norm_attn) @ w_in
    q_dil, q_mem = jnp.split(proj, [DIL_WIDTH], axis=-1)
    q_dil = _heads(q_dil, N_DIL_HEADS)
    slopes = alibi_slopes(N_DIL_HEADS)
    outs, lses = [], []
    for g, (window, dilation) in enumerate(DIL_GROUPS):
        hs = slice(g * HEADS_PER_GROUP, (g + 1) * HEADS_PER_GROUP)
        o_g, lse_g = dilated_window_attention(q_dil[:, :, hs], k_sh[:, :, hs], v_sh[:, :, hs], slopes[hs], window, dilation)
        outs.append(o_g)
        lses.append(lse_g)
    alpha = jax.nn.softmax(jnp.stack(lses, axis=0), axis=0)
    o_dil = jnp.concatenate([o * alpha[g][..., None].astype(o.dtype) for g, o in enumerate(outs)], axis=2)
    o_mem = memory_branch(q_mem, mem, norm_mem, w_mem_kv)
    x = x + jnp.concatenate([o_dil.reshape(b, s_len, DIL_WIDTH), o_mem], axis=-1) @ w_out
    return x + conv_ffn(rmsnorm(x, norm_ffn), ffn_up, ffn_conv, ffn_down)

def setup_inputs(seed: int = 0) -> dict:
    key = jax.random.key(seed)
    ks = jax.random.split(key, 24)

    def w(k, shape, fan_in):
        return jax.random.normal(k, shape, jnp.float32) * fan_in ** -0.5

    def gain(k, shape):
        return 1.0 + 0.02 * jax.random.normal(k, shape, jnp.float32)

    na, nb = N_A_LAYERS, N_B_LAYERS
    return {
        'x': jax.random.normal(ks[0], (BATCH, SEQ, D_MODEL), jnp.float32),
        'mem': jax.random.normal(ks[1], (BATCH, MEM_LEN, D_MODEL), jnp.float32),
        'a_norm_attn': gain(ks[2], (na, D_MODEL)),
        'a_w_in': w(ks[3], (na, D_MODEL, 3 * SB_WIDTH + MEM_WIDTH), D_MODEL),
        'a_w_out': w(ks[4], (na, SB_WIDTH + MEM_WIDTH, D_MODEL), SB_WIDTH + MEM_WIDTH),
        'a_norm_mem': gain(ks[5], (na, D_MODEL)),
        'a_w_mem_kv': w(ks[6], (na, D_MODEL, 2 * MEM_WIDTH), D_MODEL),
        'a_norm_ffn': gain(ks[7], (na, D_MODEL)),
        'a_ffn_up': w(ks[8], (na, D_MODEL, 2 * D_FF), D_MODEL),
        'a_ffn_conv': w(ks[9], (na, CONV_WIDTH, 2 * D_FF), CONV_WIDTH),
        'a_ffn_down': w(ks[10], (na, D_FF, D_MODEL), D_FF),
        'kv_norm': gain(ks[11], (D_MODEL,)),
        'w_kv_shared': w(ks[12], (D_MODEL, 2 * DIL_WIDTH), D_MODEL),
        'b_norm_attn': gain(ks[13], (nb, D_MODEL)),
        'b_w_in': w(ks[14], (nb, D_MODEL, DIL_WIDTH + MEM_WIDTH), D_MODEL),
        'b_w_out': w(ks[15], (nb, DIL_WIDTH + MEM_WIDTH, D_MODEL), DIL_WIDTH + MEM_WIDTH),
        'b_norm_mem': gain(ks[16], (nb, D_MODEL)),
        'b_w_mem_kv': w(ks[17], (nb, D_MODEL, 2 * MEM_WIDTH), D_MODEL),
        'b_norm_ffn': gain(ks[18], (nb, D_MODEL)),
        'b_ffn_up': w(ks[19], (nb, D_MODEL, 2 * D_FF), D_MODEL),
        'b_ffn_conv': w(ks[20], (nb, CONV_WIDTH, 2 * D_FF), CONV_WIDTH),
        'b_ffn_down': w(ks[21], (nb, D_FF, D_MODEL), D_FF),
        'final_norm': gain(ks[22], (D_MODEL,)),
    }

def reference(x, mem, a_norm_attn, a_w_in, a_w_out, a_norm_mem, a_w_mem_kv, a_norm_ffn, a_ffn_up, a_ffn_conv, a_ffn_down,
              kv_norm, w_kv_shared, b_norm_attn, b_w_in, b_w_out, b_norm_mem, b_w_mem_kv, b_norm_ffn, b_ffn_up, b_ffn_conv,
              b_ffn_down, final_norm):
    b, s_len, _ = x.shape
    h = x
    k_sh = None
    v_sh = None
    for layer in range(DEPTH):
        if layer < N_A_LAYERS:
            i = layer
            h = self_decoder_layer(h, mem, a_norm_attn[i], a_w_in[i], a_w_out[i], a_norm_mem[i], a_w_mem_kv[i],
                                   a_norm_ffn[i], a_ffn_up[i], a_ffn_conv[i], a_ffn_down[i])
            if layer == N_A_LAYERS - 1:
                k_flat, v_flat = jnp.split(rmsnorm(h, kv_norm) @ w_kv_shared, 2, axis=-1)
                k_sh = _heads(k_flat, N_DIL_HEADS)
                v_sh = _heads(v_flat, N_DIL_HEADS)
        else:
            j = layer - N_A_LAYERS
            h = cross_decoder_layer(h, k_sh, v_sh, mem, b_norm_attn[j], b_w_in[j], b_w_out[j], b_norm_mem[j],
                                    b_w_mem_kv[j], b_norm_ffn[j], b_ffn_up[j], b_ffn_conv[j], b_ffn_down[j])
    return rmsnorm(h, final_norm)


_drawn_inputs = setup_inputs


def setup_inputs(seed=0):
    import zlib

    import numpy as np

    out = dict(_drawn_inputs(seed))
    spreads = {}
    factors = {'a_norm_attn': 3.927,
     'a_norm_mem': 8.0,
     'a_norm_ffn': 3.849,
     'kv_norm': 8.0,
     'b_norm_attn': 8.0,
     'b_norm_mem': 8.0,
     'b_norm_ffn': 4.824,
     'final_norm': 2.828}
    for name, (base, spread) in spreads.items():
        noise = np.random.default_rng([zlib.crc32(name.encode()), seed]).standard_normal(out[name].shape)
        drawn = base * np.exp(spread * noise) if base else spread * noise
        out[name] = __import__('jax').numpy.asarray(drawn.astype(out[name].dtype))
    for name, factor in factors.items():
        out[name] = (out[name] * factor).astype(out[name].dtype)
    return out
```

```python
from contextlib import ExitStack

import numpy as np

import concourse.bass as bass
from concourse import mybir

F32 = mybir.dt.float32
F32R = mybir.dt.float32r
ALU = mybir.AluOpType
ACT = mybir.ActivationFunctionType
AX_X = mybir.AxisListType.X

P = 128
T = 512
D = 1024
KT = D // P
TT = T // P
M = 256
DH = 64
PAIRS = 6
MH = 4
FF = 2816
FT = FF // P
SBW = 768
EPS = 1e-6
QSCALE = DH ** -0.5
BIG = 1e30
RAW = 3
SPLIT = 2

N_MEM = 0
N_QMA = 8
N_ATA = 10
N_OUTA = 28
N_UPA = 36
N_DNA = 80
N_QMB = 102
N_ATB = 104
N_OUTB = 122
N_UPB = 130
N_DNB = 174
N_ALL = 196
B_ORDER = [0, 2, 4, 1, 3, 5]

C_NTRI, C_MASK, C_ID, C_NONE, C_D0, C_D1, C_D2, C_E = 0, 128, 256, 384, 512, 768, 896, 1024
C_ALL = 1536
CS_FROM = C_ID
G_A, G_MA, G_FA, G_KV, G_B, G_MB, G_FB, G_FIN = range(8)


def constants():
    c = np.zeros((P, C_ALL), np.float32)
    p = np.arange(P)[:, None]
    q = np.arange(P)[None, :]
    c[:, C_ID:C_ID + P] = p == q
    c[:, C_NTRI:C_NTRI + P] = -1.0 * (p >= q)
    c[:, C_MASK:C_MASK + P] = -BIG * (p >= q)
    c[:, C_NONE:C_NONE + P] = -1.0
    w = np.arange(2 * P)[None, :]
    delta = p + P - w
    c[:, C_D0:C_D0 + 2 * P] = np.where((delta >= 0) & (delta <= P), -delta, -BIG)
    c[:, C_D1:C_D1 + P] = np.where(p >= q, -4.0 * (p - q), -BIG)
    c[:, C_D2:C_D2 + P] = np.where((p >= q) & ((p - q) % 4 == 0), -4.0 * (p - q), -BIG)
    for r in range(4):
        c[:, C_E + r * P:C_E + (r + 1) * P] = q == 4 * (p % 32) + r
    return c


def slope(h):
    return 2.0 ** (-8.0 * (h + 1) / 12)


def build(nc, x, mem, a_norm_attn, a_w_in, a_w_out, a_norm_mem, a_w_mem_kv, a_norm_ffn, a_ffn_up, a_ffn_conv,
          a_ffn_down, kv_norm, w_kv_shared, b_norm_attn, b_w_in, b_w_out, b_norm_mem, b_w_mem_kv, b_norm_ffn,
          b_ffn_up, b_ffn_conv, b_ffn_down, final_norm, cst, out, stop=99):
    ctx = ExitStack()
    with ctx:
        def sb(name, shape, dt=F32):
            return ctx.enter_context(nc.sbuf_tensor(name, shape, dt))

        def sem(name):
            return ctx.enter_context(nc.semaphore(name))

        cs = sb("cs", [P, C_ALL - CS_FROM])
        cr = sb("cr", [P, 4 * P], F32R)
        hT = sb("hT", [P, KT, T])
        y_hi = sb("y_hi", [P, KT, T], F32R)
        y_lo = sb("y_lo", [P, KT, T], F32R)
        raw = sb("raw", [P, RAW, D])
        w_hi = sb("w_hi", [P, SPLIT, D], F32R)
        w_lo = sb("w_lo", [P, SPLIT, D], F32R)
        bm = sb("bm", [P, 2048], F32R)
        ar = sb("ar", [P, 22528], F32R)
        af = sb("af", [P, 4096])
        gains = sb("gains", [P, 64])
        conv = sb("conv", [P, 6 * 44])
        rT = sb("rT", [P, T])
        ss = sb("ss", [P, T])
        sq = sb("sq", [P, 2, T])
        st = sb("st", [P, 208])

        banks = [ctx.enter_context(nc.psum_tensor(f"bank{i}", [P, T], F32)) for i in range(8)]
        mem_s = [banks[2], banks[3]]
        TR = banks[7]
        OB = banks[6]

        cst_nat = hT[:, 7, :]
        ident = cs[:, C_ID - CS_FROM:C_ID - CS_FROM + P]
        nones = cs[:, C_NONE - CS_FROM:C_NONE - CS_FROM + P]
        ntri_r, mask_r, ident_r, nones_r = (cr[:, c:c + P] for c in (C_NTRI, C_MASK, C_ID, C_NONE))

        def gain(norm, k):
            return gains[:, norm * 8 + k:norm * 8 + k + 1]

        oT_hi = ar[:, 0:4096].rearrange("p (k t) -> p k t", k=KT)
        oT_lo = ar[:, 4096:8192].rearrange("p (k t) -> p k t", k=KT)
        ym = ar[:, 0:8192].rearrange("p (l s k t) -> p l s k t", l=2, s=2, k=KT)
        qk = ar[:, 8192:12288].rearrange("p (b x s t) -> p b x s t", b=2, x=2, s=2)
        vv = ar[:, 12288:14336].rearrange("p (b s k f) -> p b s k f", b=2, s=2, k=TT)
        spb = ar[:, 14336:19456].rearrange("p (b s n) -> p b s n", b=2, s=2)
        ww = ar[:, 19456:21504].rearrange("p (b s t) -> p b s t", b=2, s=2)
        qm = ar[:, 14336:16384].rearrange("p (s f t) -> p s f t", s=2, f=2)
        am = ar[:, 16896:18944]
        pmT = ar[:, 19456:21504].rearrange("p (s k t) -> p s k t", s=2, k=2)
        qmB = ar[:, 0:2048].rearrange("p (s f t) -> p s f t", s=2, f=2)
        pmTB = ar[:, 4096:6144].rearrange("p (s k t) -> p s k t", s=2, k=2)
        qkB = ar[:, 8192:10240].rearrange("p (x s t) -> p x s t", x=2, s=2)
        pT = [(ar[:, 10240:10752], ar[:, 10752:11264]), (oT_hi[:, 5, :], oT_lo[:, 5, :])]
        vB = ar[:, 19456:22528].rearrange("p (g s k f) -> p g s k f", g=3, s=2, k=TT)
        act_hi = ar[:, 0:11264].rearrange("p (k t) -> p k t", k=FT)
        act_lo = ar[:, 11264:22528].rearrange("p (k t) -> p k t", k=FT)
        km = [t[:, 0:1024].rearrange("p (s f t) -> p s f t", s=2, f=2) for t in (am, bm)]
        vm = [t[:, 1024:2048].rearrange("p (s k f) -> p s k f", s=2, k=2) for t in (am, bm)]
        x_nat = af[:, 0:4096].rearrange("p (t d) -> p t d", t=TT)
        m_nat = hT[:, 0:4, :].rearrange("p k t -> p (k t)").rearrange("p (t d) -> p t d", t=2)
        m_junk = hT[:, 4:8, :].rearrange("p k t -> p (k t)").rearrange("p (t d) -> p t d", t=2)
        qkf = af[:, 0:512]
        vT = af[:, 512:1024]
        m_vT = rT[:, 0:M]
        ze = af[:, 1024:2048].rearrange("p (b t) -> p b t", b=2)
        spf = af[:, 2048:3072].rearrange("p (b t) -> p b t", b=2)
        wf = af[:, 3072:4096].rearrange("p (b t) -> p b t", b=2)
        pm = af[:, 2048:3072]
        gv = ss[:, 3 * P:4 * P]
        cw_nat = rT
        cw2_nat = ss
        scB = af[:, 0:3840]
        biasB = af[:, 3840:4096]
        qkfs = [qkf, sq[:, 0, :]]
        vTs = [vT, sq[:, 1, :]]
        qms, pmTs = [qm, qmB], [pmT, pmTB]
        own0 = st[:, 24:40].rearrange("p (x h i) -> p x h i", x=2, h=2)
        nmax = st[:, 40:64].rearrange("p (g h r) -> p g h r", g=3, h=2)
        den = st[:, 64:88].rearrange("p (g h r) -> p g h r", g=3, h=2)
        coef = st[:, 88:112].rearrange("p (g h r) -> p g h r", g=3, h=2)
        nmin = st[:, 112:120].rearrange("p (h r) -> p h r", h=2)
        total = st[:, 120:128].rearrange("p (h r) -> p h r", h=2)
        coef0x = st[:, 128:160].rearrange("p (i h r) -> p i h r", i=4, h=2)
        coef0 = st[:, 160:168].rearrange("p (i h) -> p i h", i=4)
        smax = st[:, 168:172]
        ub = af[:, 0:1024].rearrange("p (b t) -> p b t", b=2)
        cb = af[:, 1024:2048].rearrange("p (b t) -> p b t", b=2)
        sg = af[:, 2048:2560]
        prod = af[:, 2560:3072]
        sqn = sq[:, 0, :]
        ykv_hi = ar[:, 11264:15360].rearrange("p (k t) -> p k t", k=KT)
        ykv_lo = ar[:, 15360:19456].rearrange("p (k t) -> p k t", k=KT)
        newt = sq[:, 1, :]

        ld_cst, ld_mem, ld_x, ld_g, ld_cw = (sem(n) for n in ("ld_cst", "ld_mem", "ld_x", "ld_g", "ld_cw"))
        raw_full = [sem(f"raw_full{i}") for i in range(RAW)]
        hi_done, lo_done = sem("hi_done"), sem("lo_done")
        tile_done = sem("tile_done")
        evicted = sem("evicted")
        cr_ready, tab_tr, tab_ready = sem("cr_ready"), sem("tab_tr"), sem("tab_ready")
        m_sq, m_var, m_exp, m_norm, m_tr, ym_hi, ym_lo = (sem(n) for n in ("m_sq", "m_var", "m_exp", "m_norm", "m_tr", "ym_hi", "ym_lo"))
        x_tr, h_ready, yhi, ylo, sq_done, ss_add = (sem(n) for n in ("x_tr", "h_ready", "yhi", "ylo", "sq_done", "ss_add"))
        ss_done, r_guess, r_ready = sem("ss_done"), sem("r_guess"), sem("r_ready")
        act_self, dve_self = sem("act_self"), sem("dve_self")
        kq_f, kq_hi, kq_lo = sem("kq_f"), sem("kq_hi"), sem("kq_lo")
        km_hi = sem("km_hi")
        vt_ready, vt_tr, v_hi, v_lo = sem("vt_ready"), sem("vt_tr"), sem("v_hi"), sem("v_lo")
        ms_done, mmx, mexp, mpn, mt_done, mpt_hi, mpt_lo, mav, mo_hi, mo_ev = (sem(n) for n in (
            "ms_done", "mmx", "mexp", "mpn", "mt_done", "mpt_hi", "mpt_lo", "mav", "mo_hi", "mo_ev"))
        z_done, z_min, ln_done, sp_max, sp_hi, sp_lo, cum_done, w_exp, wt_hi, wt_lo, av_done, o_hi, o_ev = (sem(n) for n in (
            "z_done", "z_min", "ln_done", "sp_max", "sp_hi", "sp_lo", "cum_done", "w_exp", "wt_hi", "wt_lo", "av_done",
            "o_hi", "o_ev"))
        tap_done, conv_half, conv_done, silu_done, prod_done, act_hi_done, act_lo_done, down_done = (sem(n) for n in (
            "tap_done", "conv_half", "conv_done", "silu_done", "prod_done", "act_hi_done", "act_lo_done", "down_done"))
        sc_done, bmax, bexp, co_gather, co_diff, co_exp, co_spread, co_back, scaled, bt_done, pt_hi, pt_lo, bav = (
            sem(n) for n in ("sc_done", "bmax", "bexp", "co_gather", "co_diff", "co_exp", "co_spread", "co_back",
                             "scaled", "bt_done", "pt_hi", "pt_lo", "bav"))
        fin_y, fin_tr, fin_ev_act, fin_ev_dve, stored = (sem(n) for n in (
            "fin_y", "fin_tr", "fin_ev_act", "fin_ev_dve", "stored"))

        selfcount = {"act": 0, "dve": 0}

        def tokens(ap, residues):
            return ap.rearrange("p (i r) -> p r i", r=4) if residues else by_tile(ap)

        def by_tile(ap):
            return ap.rearrange("p (r i) -> p r i", r=4)

        def ev_count(n):
            return n + 1 if n < N_DNA else n + 1 - 22

        U = 8 * PAIRS

        def unit(u):
            j, hp, a = u // 8, (u // 4) % 2, 3 - u % 4
            return j, hp, a, T - P * a

        SPO = [0, 512, 896, 1152]
        MEM_FILL = [(0, 5), (5, 10), (10, 15), (15, 20), (20, 24)]
        ATT_FILL = [(24 + 3 * t, 27 + 3 * t) if t < 8 * (PAIRS - 1) else None for t in range(U + 5)]
        MEM_FILL.append(None)

        def finished(fill, n0=N_ATA):
            return [n0 + s // 8 for s in range(*fill) if s % 8 == 7] if fill else []

        def score_blocks(g, hp):
            if g == 0:
                base = hp * 7 * P
                return [(base, P)] + [(base + P + 2 * P * (i - 1), 2 * P) for i in (1, 2, 3)]
            base = 14 * P + (g - 1) * 8 * P + hp * 4 * P
            return [(base + P * i, P) for i in range(4)]

        BATCHES = []
        for hp in range(2):
            b = [(score_blocks(0, hp)[i][0] + (P * (kb - i + 1) if i else 0), kb, i, kb == max(i - 1, 0), kb == i)
                 for i in range(4) for kb in range(max(i - 1, 0), i + 1)]
            BATCHES += [(0, hp, b[:3], False), (0, hp, b[3:], True)]
        for g in (1, 2):
            for hp in range(2):
                BATCHES.append((g, hp, [(score_blocks(g, hp)[i][0], i, i, True, True) for i in range(4)], True))

        def pt_buffer(jp, b):
            return 1 if b % 2 and not (jp and b == len(BATCHES) - 1) else 0

        def v_due(fills, t):
            before = fills[t - 1] if t else None
            return [(n - N_ATA) // 3 for n in finished(before) if (n - N_ATA) % 3 == 2]

        def mem_value(n):
            return 2 * (n // 4) + n % 4 - 2

        Y0 = [0, 8, 16, 32]

        FIN_DVE = (4, 6)

        def fin_evicted(q):
            before = sum(d < q for d in FIN_DVE)
            return (fin_ev_dve, before + 1) if q in FIN_DVE else (fin_ev_act, q - before + 1)

        def y_wait(e, k):
            return Y0[e] + (2 * k + 1 if e == 2 else k + 1)

        def score_bank(g, hp, i, w):
            if g == 0:
                o = (0, P, 0, 2 * P)[i]
                return banks[2 + 2 * hp + i // 2][:, o:o + w]
            return banks[2 + 2 * hp][:, P * i:P * (i + 1)]

        def out_views(jp, b):
            g, hp = BATCHES[b][:2]
            j = B_ORDER[3 * jp + g]
            a = slice(DH * hp, DH * (hp + 1))
            hd = 6 * jp + 2 * g + hp
            if g == 0:
                return oT_hi[a, j, :], oT_lo[a, j, :], OB[0:DH, :], hd
            hi, lo = (t[a, j, :].rearrange("p (i r) -> p i r", r=4) for t in (oT_hi, oT_lo))
            return hi, lo, OB[0:DH, :].rearrange("p (r i) -> p i r", r=4), hd

        def cols(w, c):
            return w[:, c:c + P].rearrange("(k p) f -> p k f", p=P)

        def tile_source(n):
            if n < N_QMA:
                return cols((a_w_mem_kv, b_w_mem_kv)[n // 4][0], P * (n % 4))
            if n < N_ATA:
                return cols(a_w_in[0], 3 * SBW + P * (n - N_QMA))
            if n < N_OUTA:
                j, s = divmod(n - N_ATA, 3)
                return cols(a_w_in[0], SBW * s + P * j)
            if n < N_UPA:
                return cols(a_w_out[0], P * (n - N_OUTA))
            if n < N_ATB:
                return cols(b_w_in[0], SBW + P * (n - N_QMB))
            if n < N_OUTB:
                j, s = divmod(n - N_ATB, 3)
                j = B_ORDER[j]
                return (cols(w_kv_shared, P * j), cols(b_w_in[0], P * j), cols(w_kv_shared, SBW + P * j))[s]
            return cols(b_w_out[0], P * (n - N_OUTB))

        block = ctx.enter_context(nc.Block())

        @block.sync
        def _(sp):
            sp.dma_start(cs[:], cst[:, CS_FROM:C_ALL]).then_inc(ld_cst, 16)
            sp.dma_start(cst_nat, cst[:, 0:4 * P]).then_inc(ld_cst, 16)
            sp.dma_start(m_nat, mem[0].rearrange("(t p) d -> p t d", p=P)).then_inc(ld_mem, 16)
            for i, g in enumerate((a_norm_attn[0], a_norm_mem[0], a_norm_ffn[0], kv_norm, b_norm_attn[0],
                                   b_norm_mem[0], b_norm_ffn[0], final_norm)):
                sp.dma_start(gv[8 * i:8 * i + 8, :], g.rearrange("(k p) -> k p", p=P)).then_inc(ld_g, 16)
            for dst, src in ((cw_nat, a_ffn_conv[0]), (cw2_nat, b_ffn_conv[0])):
                sp.dma_start(dst[0:2 * FT, 0:3 * P].rearrange("f (t p) -> f t p", t=3),
                             src.rearrange("t (f p) -> f t p", p=P)).then_inc(ld_cw, 16)

            def load(n, m, src):
                if m >= RAW:
                    sp.wait_ge(lo_done, n - (RAW - 1))
                dst = raw[:, m % RAW, :]
                if len(src.shape) == 3:
                    dst = dst.rearrange("p (k f) -> p k f", k=KT)
                sp.dma_start(dst, src).then_inc(raw_full[m % RAW], 16)

            def ffn_loads(n_up, n_dn, w_up, w_dn):
                def up(n, m, col):
                    load(n, m, w_up[:, col].rearrange("(k p) f -> p k f", p=P))
                up(n_up, n_up, slice(0, P))
                up(n_up + 1, n_up + 1, slice(FF, FF + P))
                with sp.Fori(0, 7) as i:
                    for j in range(6):
                        up(i * 6 + (n_up + 2 + j), n_up + 2 + j,
                           bass.ds(i * 3 * P + (P * (1 + j // 2) + FF * (j % 2)), P))
                for j in range(4):
                    load(n_dn + j, n_dn + j, w_dn[P * j:P * (j + 1), :])
                with sp.Fori(0, 3) as i:
                    for j in range(6):
                        load(i * 6 + (n_dn + 4 + j), n_dn + 4 + j, w_dn[bass.ds(i * 6 * P + P * (4 + j), P), :])

            for n in range(N_UPA):
                if n == 2:
                    sp.dma_start(x_nat, x[0].rearrange("(t p) d -> p t d", p=P)).then_inc(ld_x, 16)
                load(n, n, tile_source(n))
            if stop < 1:
                return
            ffn_loads(N_UPA, N_DNA, a_ffn_up[0], a_ffn_down[0])
            if stop < 2:
                return
            for n in range(N_QMB, N_UPB):
                load(n, n, tile_source(n))
            ffn_loads(N_UPB, N_DNB, b_ffn_up[0], b_ffn_down[0])
            for t in range(TT):
                for hf in range(2):
                    s, v = fin_evicted(hf * TT + t)
                    sp.wait_ge(s, v)
                    sp.dma_start(out[0, P * t:P * (t + 1), T * hf:T * (hf + 1)],
                                 x_nat[:, t, T * hf:T * (hf + 1)]).then_inc(stored, 16)
            sp.wait_ge(stored, 16 * 2 * TT)

        @block.gpsimd
        def _(pool):
            def squares(e):
                for k in range(KT):
                    c = 8 * e + k
                    pool.wait_ge(sq_done, c + 1)
                    if c:
                        pool.wait_ge(ss_add, c)
                    if k == 0:
                        if e == 0:
                            pool.wait_ge(tab_tr, 1)
                        else:
                            pool.wait_ge(ss_done, e)
                        ins = nc.gpsimd.tensor_copy(ss[:], sq[:, 0, :])
                    else:
                        ins = nc.gpsimd.tensor_tensor(ss[:], ss[:], sq[:, k % 2, :], ALU.add)
                    ins.then_inc(ss_add, 1)

            squares(0)
            for t in range(U + 2):
                if 1 <= t <= U:
                    u = t - 1
                    a, n = unit(u)[2:]
                    hd = u // 4
                    pool.wait_ge(sp_max, u + 1)
                    if hd >= 2:
                        pool.wait_ge(cum_done, 4 * (hd - 1))
                    if u == 0:
                        pool.wait_ge(mav, MH)
                    nc.gpsimd.tensor_scalar(spb[:, hd % 2, 0, SPO[a]:SPO[a] + n], spf[:, u % 2, 0:n], 1.0, 0.0,
                                            ALU.mult, ALU.add).then_inc(sp_hi, 1)
                if t >= 2:
                    u = t - 2
                    n = unit(u)[3]
                    pool.wait_ge(w_exp, u + 1)
                    if u >= 2:
                        pool.wait_ge(av_done, u - 1)
                    nc.gpsimd.tensor_scalar(ww[:, u % 2, 0, 0:n], wf[:, u % 2, 0:n], 1.0, 0.0,
                                            ALU.mult, ALU.add).then_inc(wt_hi, 1)
            squares(1)
            if stop < 1:
                return
            squares(2)
            if stop < 2:
                return
            squares(3)
            squares(4)

        @block.scalar
        def _(act):
            def link(ins):
                selfcount["act"] += 1
                ins.then_inc(act_self, 1)
                act.wait_ge(act_self, selfcount["act"])

            def ring(n, m=None, turn=0):
                m = n if m is None else m
                act.wait_ge(raw_full[m % RAW], turn * 32 + 16 * (m // RAW + 1))
                if m >= SPLIT:
                    act.wait_ge(tile_done, n - (SPLIT - 1))
                nc.scalar.activation(w_hi[:, m % SPLIT, :], raw[:, m % RAW, :], ACT.Copy).then_inc(hi_done, 1)

            def absorb(e, k):
                c = 8 * e + k
                act.wait_ge(h_ready, c + 1)
                for g, dst in (((G_A, y_hi),), ((G_FA, y_hi),), ((G_B, y_hi), (G_KV, ykv_hi)), ((G_FB, y_hi),), ())[e]:
                    nc.scalar.activation(dst[:, k, :], hT[:, k, :], ACT.Copy, scale=gain(g, k)).then_inc(yhi, 1)
                if c >= 2:
                    act.wait_ge(ss_add, c - 1)
                nc.scalar.activation(sq[:, k % 2, :], hT[:, k, :], ACT.Square).then_inc(sq_done, 1)

            def rms(e):
                act.wait_ge(ss_done, e + 1)
                link(nc.scalar.activation(newt, TR[:], ACT.Ln, scale=-1.0 / D, bias=st[:, 200:201]))
                nc.scalar.activation(rT[:], newt, ACT.Exp, scale=-0.5).then_inc(r_guess, 1)

            def v_high(iv, dst, src):
                act.wait_ge(vt_tr, iv + 1)
                nc.scalar.activation(dst, src, ACT.Copy).then_inc(v_hi, 1)

            def qk_high(i, dst, l=0):
                act.wait_ge(kq_f, i + 1)
                nc.scalar.activation(dst, qkfs[l], ACT.Copy).then_inc(kq_hi, 1)

            nc.scalar.preload_act_table_set("natural_log_exp_and_others")
            act.wait_ge(ld_cst, 32)
            nc.scalar.activation(cr[:], cst_nat, ACT.Copy).then_inc(cr_ready, 1)
            act.wait_ge(ld_mem, 16)
            act.wait_ge(cr_ready, 1)
            for t in range(2):
                nc.scalar.activation(m_junk[:, t, :], m_nat[:, t, :], ACT.Square, accum_out=st[:, t:t + 1]).then_inc(m_sq, 1)
            act.wait_ge(m_var, 1)
            link(nc.scalar.activation(st[:, 2:4], st[:, 4:6], ACT.Ln))
            nc.scalar.activation(st[:, 6:8], st[:, 2:4], ACT.Exp, scale=-0.5).then_inc(m_exp, 1)
            act.wait_ge(tab_tr, 1)
            link(nc.scalar.activation(gains[:], TR[:, 0:64], ACT.Copy))
            nc.scalar.activation(conv[:], TR[:, 64:64 + 264], ACT.Copy).then_inc(tab_ready, 1)
            ring(0)
            ring(1)
            for k in range(KT):
                act.wait_ge(m_tr, k + 1)
                for l, g in ((0, G_MA), (1, G_MB)):
                    nc.scalar.activation(ym[:, l, 0, k, :], banks[2 + k % 2][:, 0:M], ACT.Copy,
                                         scale=gain(g, k)).then_inc(ym_hi, 1)
            def mem_v_high(iv):
                l, f = divmod(iv, 2)
                v_high(iv, vm[l][:, 0, :, P * f:P * (f + 1)], TR[:, 0:M].rearrange("p (k f) -> p k f", k=2))

            for n in range(8):
                l, f = divmod(n, 4)
                ring(n + 2)
                if f < 2:
                    nc.scalar.activation(km[l][:, 0, f, :], banks[n % 2][:, 0:M], ACT.Copy).then_inc(km_hi, 1)
                if n in (3, 4, 7):
                    mem_v_high(mem_value(n - 1))
                absorb(0, n)

            def mem_exp(i):
                act.wait_ge(mmx, i + 1)
                if i:
                    act.wait_ge(mt_done, i)
                for qt in range(TT):
                    nc.scalar.activation(pm[:, M * qt:M * (qt + 1)], banks[2 + qt // 2][:, M * (qt % 2):M * (qt % 2) + M],
                                         ACT.Exp, bias=st[:, 8 + qt:9 + qt],
                                         accum_out=st[:, 12 + qt:13 + qt]).then_inc(mexp, 1)

            def mem_pt_high(i):
                act.wait_ge(mt_done, i + 1)
                if i:
                    act.wait_ge(mav, i)
                for kt in range(2):
                    nc.scalar.activation(pmTs[i // MH][:, 0, kt, :], banks[4 + kt][:], ACT.Copy).then_inc(mpt_hi, 1)

            def mem_o_high(i):
                m = i % MH
                r = DH * (m % 2)
                act.wait_ge(mav, i + 1)
                nc.scalar.activation(oT_hi[r:r + DH, 6 + m // 2, :], OB[0:DH, :], ACT.Copy).then_inc(mo_hi, 1)

            def mem_slot(l, g):
                if g >= 2:
                    mem_o_high(MH * l + g - 2)
                if 1 <= g <= MH:
                    mem_pt_high(MH * l + g - 1)
                if g < MH:
                    mem_exp(MH * l + g)

            def pair_v_high(j):
                if j >= 2:
                    act.wait_ge(av_done, 8 * (j - 1))
                v_high(4 + j, vv[:, j % 2, 0, :, :], TR[:].rearrange("p (k f) -> p k f", k=TT))

            def fill_events(fill):
                for n in finished(fill):
                    j, s = divmod(n - N_ATA, 3)
                    ring(n + 2)
                    if s < 2:
                        if j >= 2:
                            act.wait_ge(z_done, 8 * (j - 1))
                        qk_high(2 + 2 * j + s, qk[:, j % 2, s, 0, :])

            ring(N_QMA + 2)
            mem_v_high(3)
            rms(0)
            qk_high(0, qm[:, 0, 0, :])
            ring(N_QMA + 3)
            qk_high(1, qm[:, 0, 1, :])
            for g in range(6):
                mem_slot(0, g)
                for j in v_due(MEM_FILL, g):
                    pair_v_high(j)
                fill_events(MEM_FILL[g])
            for t in range(U + 5):
                if t >= 8 and t % 4 == 0:
                    hd = (t - 8) // 4
                    r = DH * (hd % 2)
                    act.wait_ge(av_done, 4 * hd + 4)
                    nc.scalar.activation(oT_hi[r:r + DH, hd // 2, :], OB[0:DH, :], ACT.Copy).then_inc(o_hi, 1)
                if t < U:
                    n = unit(t)[3]
                    act.wait_ge(z_min, t + 1)
                    link(nc.scalar.activation(ze[:, t % 2, 0:n], ze[:, t % 2, 0:n], ACT.Exp))
                    nc.scalar.activation(ze[:, t % 2, 0:n], ze[:, t % 2, 0:n], ACT.Ln, bias=1.0).then_inc(ln_done, 1)
                for j in v_due(ATT_FILL, t):
                    pair_v_high(j)
                fill_events(ATT_FILL[t])
                if 2 <= t < U + 2:
                    u = t - 2
                    n = unit(u)[3]
                    act.wait_ge(cum_done, u + 1)
                    if u >= 2:
                        act.wait_ge(wt_lo, u - 1)
                    nc.scalar.activation(wf[:, u % 2, 0:n], banks[2 + u % 4][:, 0:n], ACT.Exp).then_inc(w_exp, 1)
            for k in range(KT):
                if k < 6 or stop:
                    ring(N_OUTA + k + 2)
                absorb(1, k)

            def ffn(l, n_up, n_dn):
                def tile(c, n, m, turn, f):
                    ring(n + 2, m + 2, turn)
                    act.wait_ge(evicted, n + 1 - 22 * l)
                    nc.scalar.activation(cb[:, m % 2, :], ub[:, m % 2, :], ACT.Copy, scale=f).then_inc(tap_done, 1)

                def pair(q, n, m, turn, fa, fg):
                    if not (l == 0 and isinstance(q, int)):
                        act.wait_ge(prod_done, q + 0)
                    tile(2 * q, n, m, turn, fa)
                    tile(2 * q + 1, n + 1, m + 1, turn, fg)
                    act.wait_ge(conv_done, q * 2 + 2)
                    nc.scalar.activation(sg, cb[:, 1, :], ACT.Silu).then_inc(silu_done, 1)
                    act.wait_ge(prod_done, q + 1)
                    nc.scalar.activation(act_hi[:, q - FT * l, :] if isinstance(q, int) else
                                         act_hi[:, bass.ds(q - FT * l, 1), :], prod, ACT.Copy).then_inc(act_hi_done, 1)

                t2 = (3 * l + 2) * 2 * FT
                rms(2 * l + 1)
                nc.scalar.preload_act_table(ACT.Silu)
                pair(FT * l, n_up, n_up, 0, conv[:, t2:t2 + 1], conv[:, t2 + FT:t2 + FT + 1])
                with act.Fori(0, 7) as i:
                    for j in range(3):
                        col = i * 3 + (t2 + 1 + j)
                        pair(i * 3 + (FT * l + 1 + j), i * 6 + (n_up + 2 + 2 * j), n_up + 2 + 2 * j, i,
                             conv[:, bass.ds(col, 1)], conv[:, bass.ds(col + FT, 1)])
                ring(n_dn + 2)
                ring(n_dn + 3)
                with act.Fori(0, 3) as i:
                    for j in range(6):
                        ring(i * 6 + (n_dn + 4 + j), n_dn + 4 + j, i)
                if l == 0 and stop >= 2:
                    ring(N_QMB)
                    ring(N_QMB + 1)
                nc.scalar.preload_act_table_set("natural_log_exp_and_others")
                for k in range(KT):
                    absorb(2 * l + 2, k)

            if stop < 1:
                return
            ffn(0, N_UPA, N_DNA)
            if stop < 2:
                return

            rms(2)
            for f in range(2):
                ring(N_QMB + f + 2)
                qk_high(14 + f, qmB[:, 0, f, :], 1)

            def pair_event(jj, s):
                n = N_ATB + 3 * jj + s
                ring(n + 2)
                if s < 2:
                    if jj:
                        act.wait_ge(sc_done, 2 * jj)
                    qk_high(16 + 2 * jj + s, qkB[:, s, 0, :], 1)

            def pair_v(jj):
                if jj >= 3:
                    act.wait_ge(bav, (4, 6, 8)[jj - 3])
                v_high(10 + jj, vB[:, jj % 3, 0, :, :], TR[:].rearrange("p (k f) -> p k f", k=TT))

            for g in range(6):
                mem_slot(1, g)
                for n in finished(MEM_FILL[g], N_ATB):
                    pair_event(0, n - N_ATB)
            pair_v(0)

            def scores(jj):
                g = jj % 3
                for hp in range(2):
                    act.wait_ge(bmax, 2 * jj + hp + 1)
                    for i, (o, w) in enumerate(score_blocks(g, hp)):
                        a, b = (own0[:, 0, hp], own0[:, 1, hp]) if g == 0 else (nmax[:, g, hp], den[:, g, hp])
                        nc.scalar.activation(scB[:, o:o + w], scB[:, o:o + w], ACT.Exp, bias=a[:, i:i + 1],
                                             accum_out=b[:, i:i + 1]).then_inc(bexp, 1)

            def batch(jp, b):
                if b < len(BATCHES):
                    n = P * len(BATCHES[b][2])
                    c = 8 * jp + b
                    act.wait_ge(bt_done, c + 1)
                    if c >= 2:
                        act.wait_ge(bav, c if jp and b == 7 else c - 1)
                    nc.scalar.activation(pT[pt_buffer(jp, b)][0][:, 0:n], banks[2 + b % 4][:, 0:n],
                                         ACT.Copy).then_inc(pt_hi, 1)
                if b and BATCHES[b - 1][3]:
                    hi, lo, src, hd = out_views(jp, b - 1)
                    act.wait_ge(bav, 8 * jp + b)
                    nc.scalar.activation(hi, src, ACT.Copy).then_inc(o_hi, 1)

            for jj in range(PAIRS):
                jp, g = divmod(jj, 3)
                scores(jj)
                if g < 2:
                    for s in range(3):
                        pair_event(jj + 1, s)
                    pair_v(jj + 1)
                else:
                    if jp == 0:
                        pair_event(jj + 1, 0)
                        pair_event(jj + 1, 1)
                    act.wait_ge(co_diff, jp + 1)
                    nc.scalar.activation(st[:, 88:112], st[:, 88:112], ACT.Exp).then_inc(co_exp, 1)
                    for b in range(len(BATCHES) + 1):
                        batch(jp, b)
                        if jp == 0 and b == 5:
                            pair_event(jj + 1, 2)
                        if jp == 0 and b == 6:
                            pair_v(jj + 1)
            for k in range(KT):
                ring(N_OUTB + k + 2)
                absorb(3, k)
            ffn(1, N_UPB, N_DNB)
            rms(4)
            for q in range(2 * TT):
                if q not in FIN_DVE:
                    act.wait_ge(fin_tr, q + 1)
                    nc.scalar.activation(x_nat[:, q % TT, T * (q // TT):T * (q // TT + 1)], banks[q][:],
                                         ACT.Copy).then_inc(fin_ev_act, 1)

        @block.vector
        def _(dve):
            def link(ins):
                selfcount["dve"] += 1
                ins.then_inc(dve_self, 1)
                dve.wait_ge(dve_self, selfcount["dve"])

            def ring(n, m=None):
                m = n if m is None else m
                dve.wait_ge(hi_done, n + 1)
                nc.vector.tensor_tensor(w_lo[:, m % SPLIT, :], raw[:, m % RAW, :], w_hi[:, m % SPLIT, :].bitcast(F32),
                                        ALU.subtract).then_inc(lo_done, 1)

            def absorb_low(e, k):
                for s, (g, hi, lo) in enumerate((((G_A, y_hi, y_lo),), ((G_FA, y_hi, y_lo),),
                                                 ((G_B, y_hi, y_lo), (G_KV, ykv_hi, ykv_lo)),
                                                 ((G_FB, y_hi, y_lo),), ())[e]):
                    dve.wait_ge(yhi, y_wait(e, k) + s)
                    nc.vector.scalar_tensor_tensor(out=lo[:, k, :], in0=hT[:, k, :], scalar=gain(g, k),
                                                   in1=hi[:, k, :].bitcast(F32), op0=ALU.mult,
                                                   op1=ALU.subtract).then_inc(ylo, 1)

            def rms(e):
                dve.wait_ge(r_guess, e + 1)
                link(nc.vector.tensor_tensor(sqn, rT[:], rT[:], ALU.mult))
                link(nc.vector.tensor_scalar(newt, TR[:], -1.0 / D, EPS, ALU.mult, ALU.add))
                link(nc.vector.tensor_tensor(sqn, sqn, newt, ALU.mult))
                link(nc.vector.tensor_scalar(sqn, sqn, -0.5, 1.5, ALU.mult, ALU.add))
                ins = nc.vector.tensor_tensor(rT[:], rT[:], sqn, ALU.mult)
                ins.then_inc(r_ready, 1)
                dve.wait_ge(r_ready, e + 1)

            def v_low(iv, dst, hi, src):
                dve.wait_ge(v_hi, iv + 1)
                nc.vector.tensor_tensor(dst, src, hi.bitcast(F32), ALU.subtract).then_inc(v_lo, 1)

            nc.vector.memset(st[:, 200:201], EPS).then_inc(dve_self, 1)
            selfcount["dve"] += 1
            dve.wait_ge(m_sq, 2)
            link(nc.vector.tensor_scalar(st[:, 4:6], st[:, 0:2], 1.0 / D, EPS, ALU.mult, ALU.add))
            nc.vector.memset(st[:, 201:202], 0.0).then_inc(m_var, 1)
            dve.wait_ge(m_exp, 1)
            link(nc.vector.tensor_tensor(st[:, 0:2], st[:, 6:8], st[:, 6:8], ALU.mult))
            link(nc.vector.tensor_tensor(st[:, 0:2], st[:, 0:2], st[:, 4:6], ALU.mult))
            link(nc.vector.tensor_scalar(st[:, 0:2], st[:, 0:2], -0.5, 1.5, ALU.mult, ALU.add))
            link(nc.vector.tensor_tensor(st[:, 6:8], st[:, 6:8], st[:, 0:2], ALU.mult))
            for t in range(2):
                nc.vector.tensor_scalar(m_nat[:, t, :], m_nat[:, t, :], st[:, 6 + t:7 + t], None,
                                        ALU.mult).then_inc(m_norm, 1)
            dve.wait_ge(tab_ready, 1)
            for k in range(KT):
                for l, g in ((0, G_MA), (1, G_MB)):
                    dve.wait_ge(ym_hi, 2 * k + l + 1)
                    if l == 0:
                        dve.wait_ge(ym_hi, 2 * k + 2)
                    nc.vector.scalar_tensor_tensor(out=ym[:, l, 1, k, :], in0=banks[2 + k % 2][:, 0:M],
                                                   scalar=gain(g, k), in1=ym[:, l, 0, k, :].bitcast(F32),
                                                   op0=ALU.mult, op1=ALU.subtract).then_inc(ym_lo, 1)
                if k < 2:
                    ring(k)

            def mem_v_low(iv):
                l, f = divmod(iv, 2)
                v_low(iv, vm[l][:, 1, :, P * f:P * (f + 1)], vm[l][:, 0, :, P * f:P * (f + 1)],
                      TR[:, 0:M].rearrange("p (k f) -> p k f", k=2))

            for n in range(8):
                l, f = divmod(n, 4)
                if f >= 2:
                    dve.wait_ge(tile_done, n + 1)
                    if f == 3 or l == 1:
                        dve.wait_ge(vt_tr, 2 * l + f - 2)
                    nc.vector.tensor_copy(m_vT, banks[n % 2][:, 0:M]).then_inc(evicted, 1)
                else:
                    dve.wait_ge(km_hi, 2 * l + f + 1)
                    nc.vector.tensor_tensor(km[l][:, 1, f, :], banks[n % 2][:, 0:M], km[l][:, 0, f, :].bitcast(F32),
                                            ALU.subtract).then_inc(evicted, 1)
                ring(n + 2)
                if n in (3, 4, 7):
                    mem_v_low(mem_value(n - 1))
                if n == 0:
                    dve.wait_ge(m_tr, KT)
                dve.wait_ge(x_tr, n + 1)
                nc.vector.tensor_copy(hT[:, n, :], banks[4 + n % 2][:]).then_inc(h_ready, 1)
                absorb_low(0, n)

            def qk_float(i, n, scale, l=0, residues=False):
                dve.wait_ge(tile_done, n + 1)
                if i:
                    dve.wait_ge(kq_lo, i)
                nc.vector.scalar_tensor_tensor(out=by_tile(qkfs[l]), in0=tokens(banks[n % 2][:], residues), scalar=scale,
                                               in1=tokens(rT[:], residues), op0=ALU.mult,
                                               op1=ALU.mult).then_inc(evicted, 1)
                dve.wait_ge(evicted, ev_count(n))
                nc.vector.engine_nop().then_inc(kq_f, 1)

            def qk_low(i, dst, hi, l=0):
                dve.wait_ge(kq_hi, i + 1)
                nc.vector.tensor_tensor(dst, qkfs[l], hi.bitcast(F32), ALU.subtract).then_inc(kq_lo, 1)

            def v_float(iv, n, l=0, residues=False):
                dve.wait_ge(tile_done, n + 1)
                dve.wait_ge(vt_tr, iv)
                nc.vector.tensor_tensor(by_tile(vTs[l]), tokens(banks[n % 2][:], residues), tokens(rT[:], residues),
                                        ALU.mult).then_inc(evicted, 1)

            def mem_slot(l, g):
                if g >= 2:
                    i = MH * l + g - 2
                    m = i % MH
                    r = DH * (m % 2)
                    dve.wait_ge(mo_hi, i + 1)
                    nc.vector.tensor_tensor(oT_lo[r:r + DH, 6 + m // 2, :], OB[0:DH, :],
                                            oT_hi[r:r + DH, 6 + m // 2, :].bitcast(F32), ALU.subtract).then_inc(mo_ev, 1)
                if 1 <= g <= MH:
                    i = MH * l + g - 1
                    for kt in range(2):
                        dve.wait_ge(mpt_hi, 2 * i + kt + 1)
                        nc.vector.tensor_tensor(pmTs[l][:, 1, kt, :], banks[4 + kt][:], pmTs[l][:, 0, kt, :].bitcast(F32),
                                                ALU.subtract).then_inc(mpt_lo, 1)
                if g < MH:
                    i = MH * l + g
                    dve.wait_ge(ms_done, i + 1)
                    for b in range(2):
                        ins = nc.vector.tensor_reduce(st[:, 8 + 2 * b:10 + 2 * b], banks[2 + b][:].rearrange("p (q k) -> p q k", q=2),
                                                      AX_X, ALU.max, negate=True)
                    ins.then_inc(mmx, 1)
                    dve.wait_ge(mexp, 4 * (i + 1))
                    link(nc.vector.reciprocal(st[:, 16:20], st[:, 12:16]))
                    for qt in range(TT):
                        ins = nc.vector.tensor_scalar(pm[:, M * qt:M * (qt + 1)], pm[:, M * qt:M * (qt + 1)],
                                                      st[:, 16 + qt:17 + qt], None, ALU.mult)
                    ins.then_inc(mpn, 1)

            def pair_v_low(j):
                v_low(4 + j, vv[:, j % 2, 1, :, :], vv[:, j % 2, 0, :, :], TR[:].rearrange("p (k f) -> p k f", k=TT))

            def fill_events(fill):
                for n in finished(fill):
                    j, s = divmod(n - N_ATA, 3)
                    if s < 2:
                        qk_float(2 + 2 * j + s, n, (QSCALE, 1.0)[s])
                    else:
                        v_float(4 + j, n)
                    ring(n + 2)
                    if s < 2:
                        qk_low(2 + 2 * j + s, qk[:, j % 2, s, 1, :], qk[:, j % 2, s, 0, :])

            ring(N_QMA + 2)
            mem_v_low(3)
            rms(0)
            qk_float(0, N_QMA, QSCALE)
            qk_low(0, qm[:, 1, 0, :], qm[:, 0, 0, :])
            qk_float(1, N_QMA + 1, QSCALE)
            ring(N_QMA + 3)
            qk_low(1, qm[:, 1, 1, :], qm[:, 0, 1, :])
            for g in range(6):
                mem_slot(0, g)
                for j in v_due(MEM_FILL, g):
                    pair_v_low(j)
                fill_events(MEM_FILL[g])
            for t in range(U + 5):
                if t >= 8 and t % 4 == 0:
                    hd = (t - 8) // 4
                    r = DH * (hd % 2)
                    dve.wait_ge(o_hi, hd + 1)
                    nc.vector.tensor_tensor(oT_lo[r:r + DH, hd // 2, :], OB[0:DH, :],
                                            oT_hi[r:r + DH, hd // 2, :].bitcast(F32), ALU.subtract).then_inc(o_ev, 1)
                if t < U:
                    n = unit(t)[3]
                    dve.wait_ge(z_done, t + 1)
                    if t >= 2:
                        dve.wait_ge(sp_max, t - 1)
                    nc.vector.tensor_scalar(ze[:, t % 2, 0:n], banks[2 + t % 4][:, 0:n], 30.0, None,
                                            ALU.min).then_inc(z_min, 1)
                if 1 <= t <= U:
                    u = t - 1
                    n = unit(u)[3]
                    dve.wait_ge(ln_done, u + 1)
                    if u >= 2:
                        dve.wait_ge(sp_lo, u - 1)
                    nc.vector.tensor_tensor(spf[:, u % 2, 0:n], banks[2 + u % 4][:, 0:n], ze[:, u % 2, 0:n],
                                            ALU.max).then_inc(sp_max, 1)
                for j in v_due(ATT_FILL, t):
                    pair_v_low(j)
                fill_events(ATT_FILL[t])
                if 3 <= t < U + 3:
                    u = t - 3
                    n = unit(u)[3]
                    dve.wait_ge(wt_hi, u + 1)
                    nc.vector.tensor_tensor(ww[:, u % 2, 1, 0:n], wf[:, u % 2, 0:n], ww[:, u % 2, 0, 0:n].bitcast(F32),
                                            ALU.subtract).then_inc(wt_lo, 1)
                if 1 <= t <= U:
                    u = t - 1
                    a, n = unit(u)[2:]
                    hd = u // 4
                    dve.wait_ge(sp_hi, u + 1)
                    o = slice(SPO[a], SPO[a] + n)
                    nc.vector.tensor_tensor(spb[:, hd % 2, 1, o], spf[:, u % 2, 0:n], spb[:, hd % 2, 0, o].bitcast(F32),
                                            ALU.subtract).then_inc(sp_lo, 1)

            def out_proj(e, n0):
                for k in range(KT):
                    n = n0 + k
                    dve.wait_ge(tile_done, n + 1)
                    link(nc.vector.tensor_tensor(hT[:, k, :], hT[:, k, :], banks[n % 2][:], ALU.add))
                    nc.vector.engine_nop().then_inc(h_ready, 1)
                    nc.vector.engine_nop().then_inc(evicted, 1)
                    if n + 2 < N_UPA or stop:
                        ring(n + 2)
                    absorb_low(e, k)

            def ffn(l, n_up, n_dn):
                def tile(c, n, m, taps):
                    dve.wait_ge(tile_done, n + 1)
                    if m >= N_UPA + 2:
                        dve.wait_ge(tap_done, c - 1)
                    u, o = ub[:, m % 2, :], cb[:, m % 2, :]
                    nc.vector.tensor_tensor(u, banks[m % 2][:], rT[:], ALU.mult).then_inc(evicted, 1)
                    ring(n + 2, m + 2)
                    dve.wait_ge(tap_done, c + 1)
                    nc.vector.scalar_tensor_tensor(out=o[:, 1:T], in0=u[:, 0:T - 1], scalar=taps[1], in1=o[:, 1:T],
                                                   op0=ALU.mult, op1=ALU.add).then_inc(conv_half, 1)
                    dve.wait_ge(conv_half, c + 1)
                    nc.vector.scalar_tensor_tensor(out=o[:, 2:T], in0=u[:, 0:T - 2], scalar=taps[0], in1=o[:, 2:T],
                                                   op0=ALU.mult, op1=ALU.add).then_inc(conv_done, 1)

                def pair(q, n, m, col):
                    tile(q * 2, n, m, [col(t, 0) for t in range(2)])
                    tile(q * 2 + 1, n + 1, m + 1, [col(t, 1) for t in range(2)])
                    dve.wait_ge(conv_done, q * 2 + 2)
                    dve.wait_ge(silu_done, q + 1)
                    nc.vector.tensor_tensor(prod, cb[:, 0, :], sg, ALU.mult).then_inc(prod_done, 1)
                    dve.wait_ge(act_hi_done, q + 1)
                    k = slice(q - FT * l, q - FT * l + 1) if isinstance(q, int) else bass.ds(q - FT * l, 1)
                    nc.vector.tensor_tensor(act_lo[:, k, :], prod, act_hi[:, k, :].bitcast(F32),
                                            ALU.subtract).then_inc(act_lo_done, 1)

                base = 3 * l * 2 * FT
                rms(2 * l + 1)
                pair(FT * l, n_up, n_up, lambda t, s: conv[:, base + (2 * t + s) * FT:base + (2 * t + s) * FT + 1])
                with dve.Fori(0, 7) as i:
                    for j in range(3):
                        pair(i * 3 + (FT * l + 1 + j), i * 6 + (n_up + 2 + 2 * j), n_up + 2 + 2 * j,
                             lambda t, s: conv[:, bass.ds(i * 3 + (base + (2 * t + s) * FT + 1 + j), 1)])
                ring(n_dn + 2)
                ring(n_dn + 3)
                with dve.Fori(0, 3) as i:
                    for j in range(6):
                        ring(i * 6 + (n_dn + 4 + j), n_dn + 4 + j)
                if l == 0 and stop >= 2:
                    ring(N_QMB)
                    ring(N_QMB + 1)
                for k in range(KT):
                    if k < KT - 1:
                        dve.wait_ge(down_done, 7 * (FT * (l + 1) - 1) + k + 1)
                    else:
                        dve.wait_ge(tile_done, n_dn + FT)
                    nc.vector.tensor_tensor(hT[:, k, :], hT[:, k, :], banks[k][:], ALU.add).then_inc(h_ready, 1)
                    dve.wait_ge(h_ready, 8 * (2 * l + 2) + k + 1)
                    absorb_low(2 * l + 2, k)

            out_proj(1, N_OUTA)
            if stop < 1:
                return
            ffn(0, N_UPA, N_DNA)
            if stop < 2:
                return

            rms(2)
            for f in range(2):
                qk_float(14 + f, N_QMB + f, QSCALE, 1)
                ring(N_QMB + f + 2)
                qk_low(14 + f, qmB[:, 1, f, :], qmB[:, 0, f, :], 1)

            def pair_event(jj, s):
                n = N_ATB + 3 * jj + s
                g = jj % 3
                if s < 2:
                    qk_float(16 + 2 * jj + s, n, (1.0, QSCALE)[s], 1, g > 0)
                else:
                    v_float(10 + jj, n, 1, g > 0)
                ring(n + 2)
                if s < 2:
                    qk_low(16 + 2 * jj + s, qkB[:, s, 1, :], qkB[:, s, 0, :], 1)

            def pair_v(jj):
                v_low(10 + jj, vB[:, jj % 3, 1, :, :], vB[:, jj % 3, 0, :, :], TR[:].rearrange("p (k f) -> p k f", k=TT))

            for g in range(6):
                mem_slot(1, g)
                for n in finished(MEM_FILL[g], N_ATB):
                    pair_event(0, n - N_ATB)
            pair_v(0)

            def scores(jj):
                jp, g = divmod(jj, 3)
                for hp in range(2):
                    h = 2 * B_ORDER[jj] + hp
                    dve.wait_ge(sc_done, 2 * jj + hp + 1)
                    if jp:
                        dve.wait_ge(bt_done, (4, 6, 8)[g])
                        dve.wait_ge(co_gather, jp)
                        dve.wait_ge(co_exp, jp)
                    width = 2 * P if g == 0 else P
                    c = (C_D0, C_D1, C_D2)[g] - CS_FROM
                    link(nc.vector.tensor_scalar(biasB[:, 0:width], cs[:, c:c + width], slope(h), None, ALU.mult))
                    for i, (o, w) in enumerate(score_blocks(g, hp)):
                        link(nc.vector.tensor_tensor_reduce(
                            out=scB[:, o:o + w], in0=score_bank(g, hp, i, w), in1=biasB[:, width - w:width], scale=1.0,
                            scalar=-3e38, op0=ALU.add, op1=ALU.max, accum_out=smax[:, i:i + 1]))
                    dst = own0[:, 0, hp, :] if g == 0 else nmax[:, g, hp, :]
                    nc.vector.tensor_scalar(dst, smax, -1.0, None, ALU.mult).then_inc(bmax, 1)
                    dve.wait_ge(bmax, 2 * jj + hp + 1)

            def coefficients(jp):
                dve.wait_ge(bexp, 24 * (jp + 1))
                dve.wait_ge(co_gather, jp + 1)
                for x, dst in ((0, nmax), (1, den)):
                    link(nc.vector.tensor_copy(dst[:, 0, :, :], TR[:, 0:16].rearrange("p (r x h) -> p x h r", r=4, x=2)[:, x]))
                link(nc.vector.tensor_tensor(nmin, nmax[:, 0], nmax[:, 1], ALU.min))
                link(nc.vector.tensor_tensor(nmin, nmin, nmax[:, 2], ALU.min))
                for g in range(3):
                    ins = nc.vector.tensor_tensor(coef[:, g], nmin, nmax[:, g], ALU.subtract)
                ins.then_inc(co_diff, 1)
                dve.wait_ge(co_exp, jp + 1)
                link(nc.vector.tensor_tensor(den, den, coef, ALU.mult))
                link(nc.vector.tensor_tensor(total, den[:, 0], den[:, 1], ALU.add))
                link(nc.vector.tensor_tensor(total, total, den[:, 2], ALU.add))
                link(nc.vector.reciprocal(total, total))
                for g in range(3):
                    link(nc.vector.tensor_tensor(coef[:, g], coef[:, g], total, ALU.mult))
                link(nc.vector.memset(st[:, 128:160], 0.0))
                for i in range(4):
                    a = slice(32 * i, 32 * (i + 1))
                    ins = nc.vector.tensor_copy(coef0x[a, i], coef[a, 0])
                ins.then_inc(co_spread, 1)
                dve.wait_ge(co_back, jp + 1)
                link(nc.vector.tensor_copy(coef0, TR[:, 32:40].rearrange("p (i h) -> p i h", i=4)))
                for g in range(3):
                    for hp in range(2):
                        for i, (o, w) in enumerate(score_blocks(g, hp)):
                            c = coef0[:, i, hp:hp + 1] if g == 0 else coef[:, g, hp, i:i + 1]
                            nc.vector.tensor_scalar(scB[:, o:o + w], scB[:, o:o + w], c, None, ALU.mult).then_inc(scaled, 1)

            def batch(jp, b):
                if b < len(BATCHES):
                    n = P * len(BATCHES[b][2])
                    buf = pT[pt_buffer(jp, b)]
                    dve.wait_ge(pt_hi, 8 * jp + b + 1)
                    nc.vector.tensor_tensor(buf[1][:, 0:n], banks[2 + b % 4][:, 0:n], buf[0][:, 0:n].bitcast(F32),
                                            ALU.subtract).then_inc(pt_lo, 1)
                if b and BATCHES[b - 1][3]:
                    hi, lo, src, hd = out_views(jp, b - 1)
                    dve.wait_ge(o_hi, 12 + hd + 1)
                    nc.vector.tensor_tensor(lo, src, hi.bitcast(F32), ALU.subtract).then_inc(o_ev, 1)

            for jj in range(PAIRS):
                jp, g = divmod(jj, 3)
                scores(jj)
                if g < 2:
                    for s in range(3):
                        pair_event(jj + 1, s)
                    pair_v(jj + 1)
                else:
                    if jp == 0:
                        pair_event(jj + 1, 0)
                        pair_event(jj + 1, 1)
                    coefficients(jp)
                    for b in range(len(BATCHES) + 1):
                        batch(jp, b)
                        if jp == 0 and b == 5:
                            pair_event(jj + 1, 2)
                        if jp == 0 and b == 6:
                            pair_v(jj + 1)
            out_proj(3, N_OUTB)
            ffn(1, N_UPB, N_DNB)
            rms(4)
            for k in range(KT):
                nc.vector.scalar_tensor_tensor(out=hT[:, k, :], in0=hT[:, k, :], scalar=gain(G_FIN, k), in1=rT[:],
                                               op0=ALU.mult, op1=ALU.mult).then_inc(fin_y, 1)
            for q in FIN_DVE:
                dve.wait_ge(fin_tr, q + 1)
                nc.vector.tensor_copy(x_nat[:, q % TT, T * (q // TT):T * (q // TT + 1)], banks[q][:]).then_inc(fin_ev_dve, 1)

        @block.tensor
        def _(pe):
            mm = nc.tensor.matmul

            def steps(n, m, ks, y, y_ready=None, width=T):
                bank = banks[m % 2][:, 0:width]
                for k in ks:
                    if y_ready is not None:
                        y_ready(k)
                    w = [t[:, m % SPLIT, P * k:P * (k + 1)] for t in (w_hi, w_lo)]
                    mm(bank, w[0], y[0][:, k, :], start=(k == 0), stop=False)
                    mm(bank, w[0], y[1][:, k, :], start=False, stop=False)
                    last = mm(bank, w[1], y[0][:, k, :], start=False, stop=(k == KT - 1))
                if KT - 1 in ks:
                    last.then_inc(tile_done, 1)

            def tile(n, m, l, y, y_ready=None, width=T):
                pe.wait_ge(lo_done, n + 1)
                if m >= 2:
                    pe.wait_ge(evicted, n - 1 - 22 * l)
                steps(n, m, range(KT), y, y_ready, width)

            def sum_squares(e):
                pe.wait_ge(ss_add, 8 * (e + 1))
                if e:
                    pe.wait_ge(r_ready, e)
                pe.wait_ge(v_lo, (4, 10, 10, 16, 16)[e])
                mm(TR[:], nones, ss[:], start=True, stop=True).then_inc(ss_done, 1)

            pe.wait_ge(ld_cst, 32)
            pe.wait_ge(ld_g, 16 * 8)
            pe.wait_ge(ld_cw, 32)
            nc.tensor.transpose(TR[:, 0:64], gv[0:64, :], ident[0:64, 0:64])
            for l, nat in enumerate((cw_nat, cw2_nat)):
                for t in range(3):
                    o = 64 + (3 * l + t) * 2 * FT
                    last = nc.tensor.transpose(TR[:, o:o + 2 * FT], nat[0:2 * FT, P * t:P * (t + 1)],
                                               ident[0:2 * FT, 0:2 * FT])
            last.then_inc(tab_tr, 1)
            pe.wait_ge(m_norm, 2)
            for k in range(KT):
                if k >= 2:
                    pe.wait_ge(ym_lo, 2 * (k - 1))
                for t in range(2):
                    last = nc.tensor.transpose(banks[2 + k % 2][:, P * t:P * (t + 1)], m_nat[:, t, P * k:P * (k + 1)], ident)
                last.then_inc(m_tr, 1)

            def v_transpose(iv, count):
                pe.wait_ge(vt_ready_of(iv)[0], vt_ready_of(iv)[1])
                src = m_vT if count == 2 else vTs[iv >= 10]
                if iv:
                    pe.wait_ge(v_lo, iv)
                for t in range(count):
                    last = nc.tensor.transpose(TR[:, P * t:P * (t + 1)], src[:, P * t:P * (t + 1)], ident)
                last.then_inc(vt_tr, 1)

            def vt_ready_of(iv):
                n = (2, 3, 6, 7)[iv] if iv < 4 else (N_ATA if iv < 10 else N_ATB) + 3 * ((iv - 4) % 6) + 2
                return evicted, ev_count(n)

            pe.wait_ge(tab_ready, 1)
            for n in range(8):
                def ready(k):
                    if n == 0:
                        pe.wait_ge(ym_lo, 2 * k + 2)
                l = n // 4
                tile(n, n, 0, (ym[:, l, 0], ym[:, l, 1]), ready, M)
                if n in (3, 4, 7):
                    v_transpose(mem_value(n - 1), 2)
                pe.wait_ge(ld_x, 16)
                if n >= 2:
                    pe.wait_ge(h_ready, n - 1)
                for t in range(TT):
                    last = nc.tensor.transpose(banks[4 + n % 2][:, P * t:P * (t + 1)], x_nat[:, t, P * n:P * (n + 1)], ident)
                last.then_inc(x_tr, 1)

            y = (y_hi, y_lo)
            tile(N_QMA, N_QMA, 0, y, lambda k: pe.wait_ge(ylo, y_wait(0, k)))
            v_transpose(3, 2)
            sum_squares(0)
            tile(N_QMA + 1, N_QMA + 1, 0, y)

            def mem_scores(i, km, last_q):
                m = i % MH
                r, f = DH * (m % 2), m // 2
                pe.wait_ge(kq_lo, last_q)
                if i:
                    pe.wait_ge(mexp, 4 * i)
                for qt in range(TT):
                    o = banks[2 + qt // 2][:, M * (qt % 2):M * (qt % 2) + M]
                    for s, (a, b) in enumerate(((0, 0), (0, 1), (1, 0))):
                        last = mm(o, qms[i // MH][r:r + DH, a, f, P * qt:P * (qt + 1)], km[r:r + DH, b, f, :],
                                  start=(s == 0), stop=(s == 2))
                last.then_inc(ms_done, 1)

            def mem_transposes(i):
                pe.wait_ge(mpn, i + 1)
                if i:
                    pe.wait_ge(mpt_lo, 2 * i)
                for kt in range(2):
                    for qt in range(TT):
                        last = nc.tensor.transpose(banks[4 + kt][:, P * qt:P * (qt + 1)],
                                                   pm[:, M * qt + P * kt:M * qt + P * (kt + 1)], ident)
                last.then_inc(mt_done, 1)

            def mem_values(i, vm):
                m = i % MH
                if i:
                    pe.wait_ge(mo_ev, i)
                for kt in range(2):
                    pe.wait_ge(mpt_lo, 2 * i + kt + 1)
                    for s, (a, b) in enumerate(((0, 0), (0, 1), (1, 0))):
                        last = mm(OB[0:DH, :], vm[:, a, kt, DH * m:DH * (m + 1)], pmTs[i // MH][:, b, kt, :],
                                  start=(kt == 0 and s == 0), stop=(kt == 1 and s == 2))
                last.then_inc(mav, 1)

            def mem_slot(l, g, last_q):
                if g >= 2:
                    mem_values(MH * l + g - 2, vm[l])
                if 1 <= g <= MH:
                    mem_transposes(MH * l + g - 1)
                if g < MH:
                    mem_scores(MH * l + g, km[l], last_q)

            def fill(span):
                if not span:
                    return
                s = span[0]
                while s < span[1]:
                    n, k = N_ATA + s // 8, s % 8
                    e = min(span[1], s - k + 8)
                    if k == 0:
                        pe.wait_ge(lo_done, n + 1)
                        pe.wait_ge(evicted, n - 1)
                    steps(n, n, range(k, k + e - s), y)
                    s = e

            for g in range(6):
                mem_slot(0, g, 2)
                for j in v_due(MEM_FILL, g):
                    v_transpose(4 + j, TT)
                fill(MEM_FILL[g])

            for t in range(U + 5):
                if t < U:
                    j, hp, a, n = unit(t)
                    r = DH * hp
                    o = banks[2 + t % 4][:, 0:n]
                    if t >= 4:
                        pe.wait_ge(w_exp, t - 3)
                    else:
                        pe.wait_ge(mexp, 4 * MH)
                        pe.wait_ge(mpt_lo, 2 * MH)
                    if t % 8 == 0:
                        pe.wait_ge(kq_lo, 2 + 2 * j + 2)
                    for s, (b, c) in enumerate(((0, 0), (0, 1), (1, 0))):
                        mm(o, qk[r:r + DH, j % 2, 1, b, P * a:P * (a + 1)], qk[r:r + DH, j % 2, 0, c, P * a:T],
                           start=(s == 0), stop=False, skip_group_check=True)
                    mm(o[:, 0:P], ident_r, mask_r, start=False, stop=True, skip_group_check=True).then_inc(z_done, 1)
                for j in v_due(ATT_FILL, t):
                    v_transpose(4 + j, TT)
                fill(ATT_FILL[t])
                if 4 <= t < U + 4:
                    u = t - 4
                    j, hp, a, n = unit(u)
                    hd = u // 4
                    pe.wait_ge(wt_lo, u + 1)
                    if a == 3 and hd:
                        pe.wait_ge(o_ev, hd)
                    if u % 8 == 0:
                        pe.wait_ge(v_lo, 4 + j + 1)
                    if u == 0:
                        pe.wait_ge(mo_ev, MH)
                    for s, (b, c) in enumerate(((0, 0), (0, 1), (1, 0))):
                        last = mm(OB[0:DH, P * a:T], vv[:, j % 2, b, a, DH * hp:DH * (hp + 1)], ww[:, u % 2, c, 0:n],
                                  start=(a == 3 and s == 0), stop=(a == 0 and s == 2), skip_group_check=True)
                    last.then_inc(av_done, 1)
                if 2 <= t < U + 2:
                    u = t - 2
                    a = unit(u)[2]
                    hd = u // 4
                    pe.wait_ge(sp_lo, u + 1)
                    for b in range(3, a - 1, -1):
                        nb = T - P * b
                        for s in range(2):
                            last = mm(banks[2 + u % 4][:, P * (b - a):P * (b - a) + nb], ntri_r if b == a else nones_r,
                                      spb[:, hd % 2, s, SPO[b]:SPO[b] + nb], start=False,
                                      stop=(b == a and s == 1), skip_group_check=True)
                    last.then_inc(cum_done, 1)

            def out_proj(l, n0, e):
                pe.wait_ge(o_ev, 2 * PAIRS * (l + 1))
                pe.wait_ge(mo_ev, MH * (l + 1))
                for k in range(KT):
                    tile(n0 + k, n0 + k, l, (oT_hi, oT_lo))

            def ffn(l, n_up, n_dn):
                e = 2 * l + 1
                tile(n_up, n_up, l, y, lambda k: pe.wait_ge(ylo, y_wait(e, k)))
                sum_squares(e)
                tile(n_up + 1, n_up + 1, l, y)
                with pe.Fori(0, 7) as i:
                    for j in range(6):
                        tile(i * 6 + (n_up + 2 + j), n_up + 2 + j, l, y)

                def down(k, n, m, first):
                    pe.wait_ge(lo_done, n + 1)
                    pe.wait_ge(act_lo_done, k + (FT * l + 1))
                    kk = slice(k, k + 1) if isinstance(k, int) else bass.ds(k, 1)
                    for f in range(KT):
                        w = [t[:, m % SPLIT, P * f:P * (f + 1)] for t in (w_hi, w_lo)]
                        for s, (a, b) in enumerate(((w[0], act_hi), (w[0], act_lo), (w[1], act_hi))):
                            last = mm(banks[f][:], a, b[:, kk, :], start=(first and s == 0), stop=(s == 2),
                                      skip_group_check=True)
                        last.then_inc(down_done if f < KT - 1 else tile_done, 1)

                pe.wait_ge(evicted, ev_count(n_dn - 1))
                for k in range(4):
                    down(k, n_dn + k, n_dn + k, k == 0)
                with pe.Fori(0, 3) as i:
                    for j in range(6):
                        down(i * 6 + (4 + j), i * 6 + (n_dn + 4 + j), n_dn + 4 + j, False)

            out_proj(0, N_OUTA, 1)
            if stop < 1:
                return
            ffn(0, N_UPA, N_DNA)
            if stop < 2:
                return

            tile(N_QMB, N_QMB, 1, y, lambda k: pe.wait_ge(ylo, y_wait(2, k)))
            sum_squares(2)
            tile(N_QMB + 1, N_QMB + 1, 1, y)
            ykv = (ykv_hi, ykv_lo)

            def pair_steps(jj, s, ks=range(KT)):
                n = N_ATB + 3 * jj + s
                if 0 in ks:
                    if jj == 0 and s == 0:
                        pe.wait_ge(ylo, y_wait(2, KT - 1) + 1)
                    pe.wait_ge(lo_done, n + 1)
                    pe.wait_ge(evicted, n - 1 - 22)
                steps(n, n, ks, (ykv, y, ykv)[s])

            for g in range(6):
                mem_slot(1, g, 16)
                if MEM_FILL[g]:
                    a, b = MEM_FILL[g]
                    while a < b:
                        e = min(b, a - a % 8 + 8)
                        pair_steps(0, a // 8, range(a % 8, a % 8 + e - a))
                        a = e
            v_transpose(10, TT)

            def scores(jj):
                jp, g = divmod(jj, 3)
                pe.wait_ge(kq_lo, 16 + 2 * jj + 2)
                if jj:
                    pe.wait_ge(bmax, 2 * jj)
                else:
                    pe.wait_ge(mpt_lo, 4 * MH)
                if jp:
                    pe.wait_ge(pt_lo, 8 * jp)
                for hp in range(2):
                    r = slice(DH * hp, DH * (hp + 1))
                    for i, (_, w) in enumerate(score_blocks(g, hp)):
                        c = P * (i + 1) - w
                        for s, (a, b) in enumerate(((0, 0), (0, 1), (1, 0))):
                            last = mm(score_bank(g, hp, i, w), qkB[r, 1, a, P * i:P * (i + 1)],
                                      qkB[r, 0, b, c:c + w], start=(s == 0), stop=(s == 2))
                    last.then_inc(sc_done, 1)

            def coefficients(jp):
                pe.wait_ge(bexp, 24 * (jp + 1))
                pe.wait_ge(v_lo, (13, 16)[jp])
                for i in range(4):
                    for r in range(4):
                        last = mm(TR[32 * i:32 * (i + 1), 4 * r:4 * r + 4], ident[:, r::4], own0[:, :, :, i],
                                  start=True, stop=True)
                last.then_inc(co_gather, 1)
                pe.wait_ge(co_spread, jp + 1)
                for r in range(4):
                    c = C_E - CS_FROM + P * r
                    last = mm(TR[:, 32:40], cs[:, c:c + P], coef0x[:, :, :, r], start=(r == 0), stop=(r == 3))
                last.then_inc(co_back, 1)

            def batch_transposes(jp, b):
                blocks = BATCHES[b][2]
                pe.wait_ge(scaled, 24 * jp + sum(len(set(x[2] for x in t[2])) for t in BATCHES[:b + 1]))
                if b >= 4:
                    pe.wait_ge(pt_lo, 8 * jp + b - 3)
                for x, (o, _, _, _, _) in enumerate(blocks):
                    last = nc.tensor.transpose(banks[2 + b % 4][:, P * x:P * (x + 1)], scB[:, o:o + P], ident)
                last.then_inc(bt_done, 1)

            def batch_values(jp, b):
                g, hp, blocks, _ = BATCHES[b]
                heads = sum(t[3] for t in BATCHES[:b])
                pe.wait_ge(pt_lo, 8 * jp + b + 1)
                pe.wait_ge(v_lo, 10 + 3 * jp + g + 1)
                pe.wait_ge(o_ev, 12 + 6 * jp + heads)
                if jp == 0:
                    pe.wait_ge(mo_ev, 2 * MH)
                buf = pT[pt_buffer(jp, b)]
                for x, (_, kb, i, first, final) in enumerate(blocks):
                    for s, (c, d) in enumerate(((0, 0), (0, 1), (1, 0))):
                        last = mm(OB[0:DH, P * i:P * (i + 1)], vB[:, g, c, kb, DH * hp:DH * (hp + 1)],
                                  buf[d][:, P * x:P * (x + 1)], start=(first and s == 0), stop=(final and s == 2))
                last.then_inc(bav, 1)

            for jj in range(PAIRS):
                jp, g = divmod(jj, 3)
                scores(jj)
                if g < 2:
                    for s in range(3):
                        pair_steps(jj + 1, s)
                    v_transpose(11 + jj, TT)
                else:
                    if jp == 0:
                        pair_steps(jj + 1, 0)
                        pair_steps(jj + 1, 1)
                    coefficients(jp)
                    for b in range(len(BATCHES) + 1):
                        if b < len(BATCHES):
                            batch_transposes(jp, b)
                        if b:
                            batch_values(jp, b - 1)
                        if jp == 0 and b == 5:
                            pair_steps(jj + 1, 2)
                        if jp == 0 and b == 6:
                            v_transpose(11 + jj, TT)
            out_proj(1, N_OUTB, 3)
            ffn(1, N_UPB, N_DNB)
            sum_squares(4)
            for q in range(2 * TT):
                hf, t = divmod(q, TT)
                pe.wait_ge(fin_y, 4 * (hf + 1))
                for x in range(4):
                    last = nc.tensor.transpose(banks[q][:, P * x:P * (x + 1)], hT[:, 4 * hf + x, P * t:P * (t + 1)], ident)
                last.then_inc(fin_tr, 1)


_INS = ['x', 'mem', 'a_norm_attn', 'a_w_in', 'a_w_out', 'a_norm_mem', 'a_w_mem_kv', 'a_norm_ffn', 'a_ffn_up', 'a_ffn_conv',
        'a_ffn_down', 'kv_norm', 'w_kv_shared', 'b_norm_attn', 'b_w_in', 'b_w_out', 'b_norm_mem', 'b_w_mem_kv',
        'b_norm_ffn', 'b_ffn_up', 'b_ffn_conv', 'b_ffn_down', 'final_norm']


def kernel(**inputs):
    import concourse.bacc as bacc
    from concourse.bass_utils import run_bass_kernel_spmd

    nc = bacc.Bacc("TRN2", target_bir_lowering=False, num_devices=1)
    arrays, args = {}, []
    for name in _INS:
        arrays[f"in_{name}"] = np.ascontiguousarray(inputs[name])
    arrays["in_constants"] = constants()
    for name, a in arrays.items():
        args.append(nc.dram_tensor(name, a.shape, mybir.dt.from_np(a.dtype), kind="ExternalInput").ap())
    args.append(nc.dram_tensor("out", (1, T, D), F32, kind="ExternalOutput").ap())
    build(nc, *args)
    r = run_bass_kernel_spmd(nc, [arrays], core_ids=[0])
    return r.results[0]["out"]
```

```python
from contextlib import ExitStack

import numpy as np

import concourse.bass as bass
from concourse import mybir

F32 = mybir.dt.float32
F32R = mybir.dt.float32r
ALU = mybir.AluOpType
ACT = mybir.ActivationFunctionType
AX_X = mybir.AxisListType.X

P = 128
T = 512
D = 1024
KT = D // P
TT = T // P
M = 256
DH = 64
PAIRS = 6
MH = 4
FF = 2816
FT = FF // P
SBW = 768
EPS = 1e-6
QSCALE = DH ** -0.5
BIG = 1e30
RAW = 3
SPLIT = 2

N_MEM = 0
N_QMA = 8
N_ATA = 10
N_OUTA = 28
N_UPA = 36
N_DNA = 80
N_QMB = 102
N_ATB = 104
N_OUTB = 122
N_UPB = 130
N_DNB = 174
N_ALL = 196
B_ORDER = [0, 2, 4, 1, 3, 5]

C_NTRI, C_MASK, C_ID, C_NONE, C_D0, C_D1, C_D2, C_E = 0, 128, 256, 384, 512, 768, 896, 1024
C_ALL = 1536
CS_FROM = C_ID
G_A, G_MA, G_FA, G_KV, G_B, G_MB, G_FB, G_FIN = range(8)


def constants():
    c = np.zeros((P, C_ALL), np.float32)
    p = np.arange(P)[:, None]
    q = np.arange(P)[None, :]
    c[:, C_ID:C_ID + P] = p == q
    c[:, C_NTRI:C_NTRI + P] = -1.0 * (p >= q)
    c[:, C_MASK:C_MASK + P] = -BIG * (p >= q)
    c[:, C_NONE:C_NONE + P] = -1.0
    w = np.arange(2 * P)[None, :]
    delta = p + P - w
    c[:, C_D0:C_D0 + 2 * P] = np.where((delta >= 0) & (delta <= P), -delta, -BIG)
    c[:, C_D1:C_D1 + P] = np.where(p >= q, -4.0 * (p - q), -BIG)
    c[:, C_D2:C_D2 + P] = np.where((p >= q) & ((p - q) % 4 == 0), -4.0 * (p - q), -BIG)
    for r in range(4):
        c[:, C_E + r * P:C_E + (r + 1) * P] = q == 4 * (p % 32) + r
    return c


def slope(h):
    return 2.0 ** (-8.0 * (h + 1) / 12)


def build(nc, x, mem, a_norm_attn, a_w_in, a_w_out, a_norm_mem, a_w_mem_kv, a_norm_ffn, a_ffn_up, a_ffn_conv,
          a_ffn_down, kv_norm, w_kv_shared, b_norm_attn, b_w_in, b_w_out, b_norm_mem, b_w_mem_kv, b_norm_ffn,
          b_ffn_up, b_ffn_conv, b_ffn_down, final_norm, cst, out):
    ctx = ExitStack()
    with ctx:
        def sb(name, shape, dt=F32):
            return ctx.enter_context(nc.sbuf_tensor(name, shape, dt))

        def sem(name):
            return ctx.enter_context(nc.semaphore(name))

        cs = sb("cs", [P, C_ALL - CS_FROM])
        cr = sb("cr", [P, 4 * P], F32R)
        hT = sb("hT", [P, KT, T])
        y_hi = sb("y_hi", [P, KT, T], F32R)
        y_lo = sb("y_lo", [P, KT, T], F32R)
        raw = sb("raw", [P, RAW, D])
        w_hi = sb("w_hi", [P, SPLIT, D], F32R)
        w_lo = sb("w_lo", [P, SPLIT, D], F32R)
        bm = sb("bm", [P, 2048], F32R)
        ar = sb("ar", [P, 22528], F32R)
        af = sb("af", [P, 4096])
        gains = sb("gains", [P, 64])
        conv = sb("conv", [P, 6 * 44])
        rT = sb("rT", [P, T])
        ss = sb("ss", [P, T])
        sq = sb("sq", [P, 2, T])
        st = sb("st", [P, 208])

        banks = [ctx.enter_context(nc.psum_tensor(f"bank{i}", [P, T], F32)) for i in range(8)]
        mem_s = [banks[2], banks[3]]
        TR = banks[7]
        OB = banks[6]

        cst_nat = hT[:, 7, :]
        ident = cs[:, C_ID - CS_FROM:C_ID - CS_FROM + P]
        nones = cs[:, C_NONE - CS_FROM:C_NONE - CS_FROM + P]
        ntri_r, mask_r, ident_r, nones_r = (cr[:, c:c + P] for c in (C_NTRI, C_MASK, C_ID, C_NONE))

        def gain(norm, k):
            return gains[:, norm * 8 + k:norm * 8 + k + 1]

        oT_hi = ar[:, 0:4096].rearrange("p (k t) -> p k t", k=KT)
        oT_lo = ar[:, 4096:8192].rearrange("p (k t) -> p k t", k=KT)
        ym = ar[:, 0:8192].rearrange("p (l s k t) -> p l s k t", l=2, s=2, k=KT)
        qk = ar[:, 8192:12288].rearrange("p (b x s t) -> p b x s t", b=2, x=2, s=2)
        vv = ar[:, 12288:14336].rearrange("p (b s k f) -> p b s k f", b=2, s=2, k=TT)
        spb = ar[:, 14336:19456].rearrange("p (b s n) -> p b s n", b=2, s=2)
        ww = ar[:, 19456:21504].rearrange("p (b s t) -> p b s t", b=2, s=2)
        qm = ar[:, 14336:16384].rearrange("p (s f t) -> p s f t", s=2, f=2)
        am = ar[:, 16896:18944]
        pmT = ar[:, 19456:21504].rearrange("p (s k t) -> p s k t", s=2, k=2)
        qmB = ar[:, 0:2048].rearrange("p (s f t) -> p s f t", s=2, f=2)
        pmTB = ar[:, 4096:6144].rearrange("p (s k t) -> p s k t", s=2, k=2)
        qkB = ar[:, 8192:10240].rearrange("p (x s t) -> p x s t", x=2, s=2)
        pT = [(ar[:, 10240:10752], ar[:, 10752:11264]), (oT_hi[:, 5, :], oT_lo[:, 5, :])]
        vB = ar[:, 19456:22528].rearrange("p (g s k f) -> p g s k f", g=3, s=2, k=TT)
        act_hi = ar[:, 0:11264].rearrange("p (k t) -> p k t", k=FT)
        act_lo = ar[:, 11264:22528].rearrange("p (k t) -> p k t", k=FT)
        km = [t[:, 0:1024].rearrange("p (s f t) -> p s f t", s=2, f=2) for t in (am, bm)]
        vm = [t[:, 1024:2048].rearrange("p (s k f) -> p s k f", s=2, k=2) for t in (am, bm)]
        x_nat = af[:, 0:4096].rearrange("p (t d) -> p t d", t=TT)
        m_nat = hT[:, 0:4, :].rearrange("p k t -> p (k t)").rearrange("p (t d) -> p t d", t=2)
        m_junk = hT[:, 4:8, :].rearrange("p k t -> p (k t)").rearrange("p (t d) -> p t d", t=2)
        qkf = af[:, 0:512]
        vT = af[:, 512:1024]
        m_vT = rT[:, 0:M]
        ze = af[:, 1024:2048].rearrange("p (b t) -> p b t", b=2)
        spf = af[:, 2048:3072].rearrange("p (b t) -> p b t", b=2)
        wf = af[:, 3072:4096].rearrange("p (b t) -> p b t", b=2)
        pm = af[:, 2048:3072]
        gv = ss[:, 3 * P:4 * P]
        cw_nat = rT
        cw2_nat = ss
        scB = af[:, 0:3840]
        biasB = af[:, 3840:4096]
        qkfs = [qkf, sq[:, 0, :]]
        vTs = [vT, sq[:, 1, :]]
        qms, pmTs = [qm, qmB], [pmT, pmTB]
        own0 = st[:, 24:40].rearrange("p (x h i) -> p x h i", x=2, h=2)
        nmax = st[:, 40:64].rearrange("p (g h r) -> p g h r", g=3, h=2)
        den = st[:, 64:88].rearrange("p (g h r) -> p g h r", g=3, h=2)
        coef = st[:, 88:112].rearrange("p (g h r) -> p g h r", g=3, h=2)
        nmin = st[:, 112:120].rearrange("p (h r) -> p h r", h=2)
        total = st[:, 120:128].rearrange("p (h r) -> p h r", h=2)
        coef0x = st[:, 128:160].rearrange("p (i h r) -> p i h r", i=4, h=2)
        coef0 = st[:, 160:168].rearrange("p (i h) -> p i h", i=4)
        smax = st[:, 168:172]
        ub = af[:, 0:1024].rearrange("p (b t) -> p b t", b=2)
        cb = af[:, 1024:2048].rearrange("p (b t) -> p b t", b=2)
        sg = af[:, 2048:2560]
        prod = af[:, 2560:3072]
        sqn = sq[:, 0, :]
        ykv_hi = ar[:, 11264:15360].rearrange("p (k t) -> p k t", k=KT)
        ykv_lo = ar[:, 15360:19456].rearrange("p (k t) -> p k t", k=KT)
        newt = sq[:, 1, :]

        ld_cst, ld_mem, ld_x, ld_g, ld_cw = (sem(n) for n in ("ld_cst", "ld_mem", "ld_x", "ld_g", "ld_cw"))
        raw_full = [sem(f"raw_full{i}") for i in range(RAW)]
        hi_done, lo_done = sem("hi_done"), sem("lo_done")
        tile_done = sem("tile_done")
        evicted = sem("evicted")
        cr_ready, tab_tr, tab_ready = sem("cr_ready"), sem("tab_tr"), sem("tab_ready")
        m_sq, m_var, m_exp, m_norm, m_tr, ym_hi, ym_lo = (sem(n) for n in ("m_sq", "m_var", "m_exp", "m_norm", "m_tr", "ym_hi", "ym_lo"))
        x_tr, h_ready, yhi, ylo, sq_done, ss_add = (sem(n) for n in ("x_tr", "h_ready", "yhi", "ylo", "sq_done", "ss_add"))
        ss_done, r_guess, r_ready = sem("ss_done"), sem("r_guess"), sem("r_ready")
        act_self, dve_self = sem("act_self"), sem("dve_self")
        kq_f, kq_hi, kq_lo = sem("kq_f"), sem("kq_hi"), sem("kq_lo")
        km_hi = sem("km_hi")
        vt_ready, vt_tr, v_hi, v_lo = sem("vt_ready"), sem("vt_tr"), sem("v_hi"), sem("v_lo")
        ms_done, mmx, mexp, mpn, mt_done, mpt_hi, mpt_lo, mav, mo_hi, mo_ev = (sem(n) for n in (
            "ms_done", "mmx", "mexp", "mpn", "mt_done", "mpt_hi", "mpt_lo", "mav", "mo_hi", "mo_ev"))
        z_done, z_min, ln_done, sp_max, sp_hi, sp_lo, cum_done, w_exp, wt_hi, wt_lo, av_done, o_hi, o_ev = (sem(n) for n in (
            "z_done", "z_min", "ln_done", "sp_max", "sp_hi", "sp_lo", "cum_done", "w_exp", "wt_hi", "wt_lo", "av_done",
            "o_hi", "o_ev"))
        tap_done, conv_half, conv_done, silu_done, prod_done, act_hi_done, act_lo_done, down_done = (sem(n) for n in (
            "tap_done", "conv_half", "conv_done", "silu_done", "prod_done", "act_hi_done", "act_lo_done", "down_done"))
        sc_done, bmax, bexp, co_gather, co_diff, co_exp, co_spread, co_back, scaled, bt_done, pt_hi, pt_lo, bav = (
            sem(n) for n in ("sc_done", "bmax", "bexp", "co_gather", "co_diff", "co_exp", "co_spread", "co_back",
                             "scaled", "bt_done", "pt_hi", "pt_lo", "bav"))
        fin_sq, fin_g, fin_tr, fin_guess, fin_ready, fin_ev_act, fin_ev_dve, stored = (sem(n) for n in (
            "fin_sq", "fin_g", "fin_tr", "fin_guess", "fin_ready", "fin_ev_act", "fin_ev_dve", "stored"))

        selfcount = {"act": 0, "dve": 0}

        def tokens(ap, residues):
            return ap.rearrange("p (i r) -> p r i", r=4) if residues else by_tile(ap)

        def by_tile(ap):
            return ap.rearrange("p (r i) -> p r i", r=4)

        def ev_count(n):
            return n + 1 if n < N_DNA else n + 1 - 22

        U = 8 * PAIRS

        def unit(u):
            j, hp, a = u // 8, (u // 4) % 2, 3 - u % 4
            return j, hp, a, T - P * a

        SPO = [0, 512, 896, 1152]
        MEM_FILL = [(0, 5), (5, 10), (10, 15), (15, 20), (20, 24)]
        ATT_FILL = [(24 + 3 * t, 27 + 3 * t) if t < 8 * (PAIRS - 1) else None for t in range(U + 5)]
        MEM_FILL.append(None)
        MEM_FILL_B = [(5, 10), (10, 15), (15, 20), (20, 24), None, None]

        def finished(fill, n0=N_ATA):
            return [n0 + s // 8 for s in range(*fill) if s % 8 == 7] if fill else []

        def score_blocks(g, hp):
            if g == 0:
                base = hp * 7 * P
                return [(base, P)] + [(base + P + 2 * P * (i - 1), 2 * P) for i in (1, 2, 3)]
            base = 14 * P + (g - 1) * 8 * P + hp * 4 * P
            return [(base + P * i, P) for i in range(4)]

        BATCHES = []
        for hp in range(2):
            b = [(score_blocks(0, hp)[i][0] + (P * (kb - i + 1) if i else 0), kb, i, kb == max(i - 1, 0), kb == i)
                 for i in range(4) for kb in range(max(i - 1, 0), i + 1)]
            BATCHES += [(0, hp, b[:3], False), (0, hp, b[3:], True)]
        for g in (1, 2):
            for hp in range(2):
                BATCHES.append((g, hp, [(score_blocks(g, hp)[i][0], i, i, True, True) for i in range(4)], True))

        SEQ_B = [("S", 0), ("P", 1, 0), ("P", 1, 1), ("P", 1, 2), ("V", 1), ("S", 1), ("P", 2, 0), ("P", 2, 1), ("P", 2, 2),
                 ("V", 2), ("S", 2), ("P", 3, 0), ("G", 0), ("P", 3, 1), ("R", 0),
                 ("T", 0, 0), ("T", 0, 1), ("A", 0, 0), ("T", 0, 2), ("A", 0, 1), ("T", 0, 3), ("A", 0, 2), ("A", 0, 3),
                 ("P", 3, 2), ("V", 3), ("S", 3),
                 ("P", 4, 0), ("T", 0, 4), ("T", 0, 5), ("A", 0, 4), ("P", 4, 1), ("A", 0, 5), ("P", 4, 2), ("V", 4), ("S", 4),
                 ("P", 5, 0), ("T", 0, 6), ("T", 0, 7), ("A", 0, 6), ("P", 5, 1), ("A", 0, 7), ("P", 5, 2), ("V", 5), ("S", 5)]
        OUT_B = [(N_OUTB + x, k) for x in range(2) for k in [6, 7] + B_ORDER[:3]]
        SEQ_B += [("O",) + t for t in OUT_B[0:3]] + [("G", 1)] + [("O",) + t for t in OUT_B[3:7]] + [("R", 1)]
        left = [("O",) + t for t in OUT_B[7:]] + [("O", N_OUTB, B_ORDER[3]), ("O", N_OUTB + 1, B_ORDER[3])]
        for b in range(9):
            SEQ_B += ([("T", 1, b)] if b < 8 else []) + ([("A", 1, b - 1)] if b else [])
            if b in (0, 1, 2, 5, 6):
                SEQ_B.append(left.pop(0))
        OUT_B = [t[1:] for t in SEQ_B if t[0] == "O"]

        def pt_buffer(jp, b):
            return 1 if b % 2 and not (jp and b == len(BATCHES) - 1) else 0

        OUT_KS = [[6, 7] + list(range(PAIRS)), [6, 7] + B_ORDER]
        OUT_FILL = [(N_OUTA + x, k) for ks in (OUT_KS[0][:6], OUT_KS[0][6:7]) for x in range(2) for k in ks]
        OUT_SLOT = {8 * (PAIRS - 1) + i // 2: OUT_FILL[i:i + 2] for i in range(0, len(OUT_FILL), 2)}

        def v_due(fills, t):
            before = fills[t - 1] if t else None
            return [(n - N_ATA) // 3 for n in finished(before) if (n - N_ATA) % 3 == 2]

        def mem_value(n):
            return 2 * (n // 4) + n % 4 - 2

        Y0 = [0, 8, 16, 32]

        YM_BANK = (banks[2], banks[3], OB)

        FIN_DVE = (1, 3, 5, 7)
        FIN_BANK = (1, 2, 3, 4, 5, 6, 7, 1)
        fin_ss = banks[0][:, 0:TT]
        fin_r = st[:, 172:176]
        fin_t = st[:, 176:180]
        fin_v = st[:, 180:184]

        def fin_evicted(q):
            before = sum(d < q for d in FIN_DVE)
            return (fin_ev_dve, before + 1) if q in FIN_DVE else (fin_ev_act, q - before + 1)

        def y_wait(e, k):
            return Y0[e] + k + 1

        def ykv_wait(k):
            return Y0[2] + KT + k + 1

        def score_bank(g, hp, i, w):
            if g == 0:
                o = (0, P, 0, 2 * P)[i]
                return banks[2 + 2 * hp + i // 2][:, o:o + w]
            return banks[2 + 2 * hp][:, P * i:P * (i + 1)]

        def out_views(jp, b):
            g, hp = BATCHES[b][:2]
            j = B_ORDER[3 * jp + g]
            a = slice(DH * hp, DH * (hp + 1))
            hd = 6 * jp + 2 * g + hp
            if g == 0:
                return oT_hi[a, j, :], oT_lo[a, j, :], OB[0:DH, :], hd
            hi, lo = (t[a, j, :].rearrange("p (i r) -> p i r", r=4) for t in (oT_hi, oT_lo))
            return hi, lo, OB[0:DH, :].rearrange("p (r i) -> p i r", r=4), hd

        def cols(w, c):
            return w[:, c:c + P].rearrange("(k p) f -> p k f", p=P)

        def tile_source(n):
            if n < N_QMA:
                return cols((a_w_mem_kv, b_w_mem_kv)[n // 4][0], P * (n % 4))
            if n < N_ATA:
                return cols(a_w_in[0], 3 * SBW + P * (n - N_QMA))
            if n < N_OUTA:
                j, s = divmod(n - N_ATA, 3)
                return cols(a_w_in[0], SBW * s + P * j)
            if n < N_UPA:
                return cols(a_w_out[0], P * (n - N_OUTA))
            if n < N_ATB:
                return cols(b_w_in[0], SBW + P * (n - N_QMB))
            if n < N_OUTB:
                j, s = divmod(n - N_ATB, 3)
                j = B_ORDER[j]
                return (cols(w_kv_shared, P * j), cols(b_w_in[0], P * j), cols(w_kv_shared, SBW + P * j))[s]
            return cols(b_w_out[0], P * (n - N_OUTB))

        block = ctx.enter_context(nc.Block())

        @block.sync
        def _(sp):
            sp.dma_start(cs[:], cst[:, CS_FROM:C_ALL]).then_inc(ld_cst, 16)
            sp.dma_start(cst_nat, cst[:, 0:4 * P]).then_inc(ld_cst, 16)
            sp.dma_start(m_nat, mem[0].rearrange("(t p) d -> p t d", p=P)).then_inc(ld_mem, 16)
            for i, g in enumerate((a_norm_attn[0], a_norm_mem[0], a_norm_ffn[0], kv_norm, b_norm_attn[0],
                                   b_norm_mem[0], b_norm_ffn[0], final_norm)):
                sp.dma_start(gv[8 * i:8 * i + 8, :], g.rearrange("(k p) -> k p", p=P)).then_inc(ld_g, 16)
            for dst, src in ((cw_nat, a_ffn_conv[0]), (cw2_nat, b_ffn_conv[0])):
                sp.dma_start(dst[0:2 * FT, 0:3 * P].rearrange("f (t p) -> f t p", t=3),
                             src.rearrange("t (f p) -> f t p", p=P)).then_inc(ld_cw, 16)

            def load(n, m, src):
                if m >= RAW:
                    sp.wait_ge(lo_done, n - (RAW - 1))
                dst = raw[:, m % RAW, :]
                if len(src.shape) == 3:
                    dst = dst.rearrange("p (k f) -> p k f", k=KT)
                sp.dma_start(dst, src).then_inc(raw_full[m % RAW], 16)

            def ffn_loads(n_up, n_dn, w_up, w_dn):
                def up(n, m, col):
                    load(n, m, w_up[:, col].rearrange("(k p) f -> p k f", p=P))
                up(n_up, n_up, slice(0, P))
                up(n_up + 1, n_up + 1, slice(FF, FF + P))
                with sp.Fori(0, 7) as i:
                    for j in range(6):
                        up(i * 6 + (n_up + 2 + j), n_up + 2 + j,
                           bass.ds(i * 3 * P + (P * (1 + j // 2) + FF * (j % 2)), P))
                for j in range(4):
                    load(n_dn + j, n_dn + j, w_dn[P * j:P * (j + 1), :])
                with sp.Fori(0, 3) as i:
                    for j in range(6):
                        load(i * 6 + (n_dn + 4 + j), n_dn + 4 + j, w_dn[bass.ds(i * 6 * P + P * (4 + j), P), :])

            for n in range(N_UPA):
                if n == 2:
                    sp.dma_start(x_nat, x[0].rearrange("(t p) d -> p t d", p=P)).then_inc(ld_x, 16)
                load(n, n, tile_source(n))
            ffn_loads(N_UPA, N_DNA, a_ffn_up[0], a_ffn_down[0])
            for n in range(N_QMB, N_UPB):
                load(n, n, tile_source(n))
            ffn_loads(N_UPB, N_DNB, b_ffn_up[0], b_ffn_down[0])
            for t in range(TT):
                for hf in range(2):
                    s, v = fin_evicted(hf * TT + t)
                    sp.wait_ge(s, v)
                    sp.dma_start(out[0, P * t:P * (t + 1), T * hf:T * (hf + 1)],
                                 x_nat[:, t, T * hf:T * (hf + 1)]).then_inc(stored, 16)
            sp.wait_ge(stored, 16 * 2 * TT)

        @block.gpsimd
        def _(pool):
            def squares(e):
                for k in range(KT):
                    c = 8 * e + k
                    pool.wait_ge(sq_done, c + 1)
                    if c:
                        pool.wait_ge(ss_add, c)
                    if k == 0:
                        if e == 0:
                            pool.wait_ge(tab_tr, 1)
                        else:
                            pool.wait_ge(ss_done, e)
                        ins = nc.gpsimd.tensor_copy(ss[:], sq[:, 0, :])
                    else:
                        ins = nc.gpsimd.tensor_tensor(ss[:], ss[:], sq[:, k % 2, :], ALU.add)
                    ins.then_inc(ss_add, 1)

            squares(0)
            for t in range(U + 2):
                if 1 <= t <= U:
                    u = t - 1
                    a, n = unit(u)[2:]
                    hd = u // 4
                    pool.wait_ge(sp_max, u + 1)
                    if hd >= 2:
                        pool.wait_ge(cum_done, 4 * (hd - 1))
                    if u == 0:
                        pool.wait_ge(mav, MH)
                    nc.gpsimd.tensor_scalar(spb[:, hd % 2, 0, SPO[a]:SPO[a] + n], spf[:, u % 2, 0:n], 1.0, 0.0,
                                            ALU.mult, ALU.add).then_inc(sp_hi, 1)
                if t >= 2:
                    u = t - 2
                    n = unit(u)[3]
                    pool.wait_ge(w_exp, u + 1)
                    if u >= 2:
                        pool.wait_ge(av_done, u - 1)
                    nc.gpsimd.tensor_scalar(ww[:, u % 2, 0, 0:n], wf[:, u % 2, 0:n], 1.0, 0.0,
                                            ALU.mult, ALU.add).then_inc(wt_hi, 1)
            squares(1)
            squares(2)
            squares(3)

        @block.scalar
        def _(act):
            def link(ins):
                selfcount["act"] += 1
                ins.then_inc(act_self, 1)
                act.wait_ge(act_self, selfcount["act"])

            def ring(n, m=None, turn=0):
                m = n if m is None else m
                act.wait_ge(raw_full[m % RAW], turn * 32 + 16 * (m // RAW + 1))
                if m >= SPLIT:
                    act.wait_ge(tile_done, n - (SPLIT - 1))
                nc.scalar.activation(w_hi[:, m % SPLIT, :], raw[:, m % RAW, :], ACT.Copy).then_inc(hi_done, 1)

            def absorb(e, k):
                c = 8 * e + k
                act.wait_ge(h_ready, c + 1)
                g = (G_A, G_FA, G_B, G_FB)[e]
                nc.scalar.activation(y_hi[:, k, :], hT[:, k, :], ACT.Copy, scale=gain(g, k)).then_inc(yhi, 1)
                if c >= 2:
                    act.wait_ge(ss_add, c - 1)
                nc.scalar.activation(sq[:, k % 2, :], hT[:, k, :], ACT.Square).then_inc(sq_done, 1)

            def rms(e):
                act.wait_ge(ss_done, e + 1)
                link(nc.scalar.activation(newt, TR[:], ACT.Ln, scale=-1.0 / D, bias=st[:, 200:201]))
                nc.scalar.activation(rT[:], newt, ACT.Exp, scale=-0.5).then_inc(r_guess, 1)

            def v_high(iv, dst, src):
                act.wait_ge(vt_tr, iv + 1)
                nc.scalar.activation(dst, src, ACT.Copy).then_inc(v_hi, 1)

            def qk_high(i, dst, l=0):
                act.wait_ge(kq_f, i + 1)
                nc.scalar.activation(dst, qkfs[l], ACT.Copy).then_inc(kq_hi, 1)

            nc.scalar.preload_act_table_set("natural_log_exp_and_others")
            act.wait_ge(ld_cst, 32)
            nc.scalar.activation(cr[:], cst_nat, ACT.Copy).then_inc(cr_ready, 1)
            act.wait_ge(ld_mem, 16)
            act.wait_ge(cr_ready, 1)
            for t in range(2):
                nc.scalar.activation(m_junk[:, t, :], m_nat[:, t, :], ACT.Square, accum_out=st[:, t:t + 1]).then_inc(m_sq, 1)
            act.wait_ge(m_var, 1)
            link(nc.scalar.activation(st[:, 2:4], st[:, 4:6], ACT.Ln))
            nc.scalar.activation(st[:, 6:8], st[:, 2:4], ACT.Exp, scale=-0.5).then_inc(m_exp, 1)
            act.wait_ge(tab_tr, 1)
            link(nc.scalar.activation(gains[:], TR[:, 0:64], ACT.Copy))
            nc.scalar.activation(conv[:], TR[:, 64:64 + 264], ACT.Copy).then_inc(tab_ready, 1)
            ring(0)
            ring(1)
            for k in range(KT):
                act.wait_ge(m_tr, k + 1)
                for l, g in ((0, G_MA), (1, G_MB)):
                    nc.scalar.activation(ym[:, l, 0, k, :], YM_BANK[k % 3][:, 0:M], ACT.Copy,
                                         scale=gain(g, k)).then_inc(ym_hi, 1)
            def mem_v_high(iv):
                l, f = divmod(iv, 2)
                v_high(iv, vm[l][:, 0, :, P * f:P * (f + 1)], TR[:, 0:M].rearrange("p (k f) -> p k f", k=2))

            for n in range(8):
                l, f = divmod(n, 4)
                ring(n + 2)
                if f < 2:
                    nc.scalar.activation(km[l][:, 0, f, :], banks[n % 2][:, 0:M], ACT.Copy).then_inc(km_hi, 1)
                if n in (3, 4, 7):
                    mem_v_high(mem_value(n - 1))
                absorb(0, n)

            def mem_exp(i):
                act.wait_ge(mmx, i + 1)
                if i:
                    act.wait_ge(mt_done, i)
                for qt in range(TT):
                    nc.scalar.activation(pm[:, M * qt:M * (qt + 1)], banks[2 + qt // 2][:, M * (qt % 2):M * (qt % 2) + M],
                                         ACT.Exp, bias=st[:, 8 + qt:9 + qt],
                                         accum_out=st[:, 12 + qt:13 + qt]).then_inc(mexp, 1)

            def mem_pt_high(i):
                act.wait_ge(mt_done, i + 1)
                if i:
                    act.wait_ge(mav, i)
                for kt in range(2):
                    nc.scalar.activation(pmTs[i // MH][:, 0, kt, :], banks[4 + kt][:], ACT.Copy).then_inc(mpt_hi, 1)

            def mem_o_high(i):
                m = i % MH
                r = DH * (m % 2)
                act.wait_ge(mav, i + 1)
                nc.scalar.activation(oT_hi[r:r + DH, 6 + m // 2, :], OB[0:DH, :], ACT.Copy).then_inc(mo_hi, 1)

            def mem_slot(l, g):
                if g >= 2:
                    mem_o_high(MH * l + g - 2)
                if 1 <= g <= MH:
                    mem_pt_high(MH * l + g - 1)
                if g < MH:
                    mem_exp(MH * l + g)

            def pair_v_high(j):
                if j >= 2:
                    act.wait_ge(av_done, 8 * (j - 1))
                v_high(4 + j, vv[:, j % 2, 0, :, :], TR[:].rearrange("p (k f) -> p k f", k=TT))

            def fill_events(fill):
                for n in finished(fill):
                    j, s = divmod(n - N_ATA, 3)
                    ring(n + 2)
                    if s < 2:
                        if j >= 2:
                            act.wait_ge(z_done, 8 * (j - 1))
                        qk_high(2 + 2 * j + s, qk[:, j % 2, s, 0, :])

            ring(N_QMA + 2)
            mem_v_high(3)
            rms(0)
            qk_high(0, qm[:, 0, 0, :])
            ring(N_QMA + 3)
            qk_high(1, qm[:, 0, 1, :])
            for g in range(6):
                mem_slot(0, g)
                for j in v_due(MEM_FILL, g):
                    pair_v_high(j)
                fill_events(MEM_FILL[g])
            for t in range(U + 5):
                if t >= 8 and t % 4 == 0:
                    hd = (t - 8) // 4
                    r = DH * (hd % 2)
                    act.wait_ge(av_done, 4 * hd + 4)
                    nc.scalar.activation(oT_hi[r:r + DH, hd // 2, :], OB[0:DH, :], ACT.Copy).then_inc(o_hi, 1)
                if t < U:
                    n = unit(t)[3]
                    act.wait_ge(z_min, t + 1)
                    link(nc.scalar.activation(ze[:, t % 2, 0:n], ze[:, t % 2, 0:n], ACT.Exp))
                    nc.scalar.activation(ze[:, t % 2, 0:n], ze[:, t % 2, 0:n], ACT.Ln, bias=1.0).then_inc(ln_done, 1)
                for j in v_due(ATT_FILL, t):
                    pair_v_high(j)
                fill_events(ATT_FILL[t])
                if 2 <= t < U + 2:
                    u = t - 2
                    n = unit(u)[3]
                    act.wait_ge(cum_done, u + 1)
                    if u >= 2:
                        act.wait_ge(wt_lo, u - 1)
                    nc.scalar.activation(wf[:, u % 2, 0:n], banks[2 + u % 4][:, 0:n], ACT.Exp).then_inc(w_exp, 1)
            for k in range(KT):
                ring(N_OUTA + k + 2)
                absorb(1, k)

            def ffn(l, n_up, n_dn):
                def tile(c, n, m, turn, f):
                    ring(n + 2, m + 2, turn)
                    act.wait_ge(evicted, n + 1 - 22 * l)
                    nc.scalar.activation(cb[:, m % 2, :], ub[:, m % 2, :], ACT.Copy, scale=f).then_inc(tap_done, 1)

                def pair(q, n, m, turn, fa, fg):
                    if not (l == 0 and isinstance(q, int)):
                        act.wait_ge(prod_done, q + 0)
                    tile(2 * q, n, m, turn, fa)
                    tile(2 * q + 1, n + 1, m + 1, turn, fg)
                    act.wait_ge(conv_done, q * 2 + 2)
                    nc.scalar.activation(sg, cb[:, 1, :], ACT.Silu).then_inc(silu_done, 1)
                    act.wait_ge(prod_done, q + 1)
                    nc.scalar.activation(act_hi[:, q - FT * l, :] if isinstance(q, int) else
                                         act_hi[:, bass.ds(q - FT * l, 1), :], prod, ACT.Copy).then_inc(act_hi_done, 1)

                t2 = (3 * l + 2) * 2 * FT
                rms(2 * l + 1)
                nc.scalar.preload_act_table(ACT.Silu)
                pair(FT * l, n_up, n_up, 0, conv[:, t2:t2 + 1], conv[:, t2 + FT:t2 + FT + 1])
                with act.Fori(0, 7) as i:
                    for j in range(3):
                        col = i * 3 + (t2 + 1 + j)
                        pair(i * 3 + (FT * l + 1 + j), i * 6 + (n_up + 2 + 2 * j), n_up + 2 + 2 * j, i,
                             conv[:, bass.ds(col, 1)], conv[:, bass.ds(col + FT, 1)])
                nc.scalar.preload_act_table_set("natural_log_exp_and_others")
                ring(n_dn + 2)
                ring(n_dn + 3)
                with act.Fori(0, 3) as i:
                    for j in range(6):
                        ring(i * 6 + (n_dn + 4 + j), n_dn + 4 + j, i)
                if l == 0:
                    ring(N_QMB)
                    for k in range(KT):
                        absorb(2, k)
                        if k == 3:
                            ring(N_QMB + 1)

            ffn(0, N_UPA, N_DNA)

            def shared_high(ks):
                for k in ks:
                    nc.scalar.activation(ykv_hi[:, k, :], hT[:, k, :], ACT.Copy, scale=gain(G_KV, k)).then_inc(yhi, 1)

            shared_high(range(4))
            rms(2)
            shared_high(range(4, KT))
            for f in range(2):
                ring(N_QMB + f + 2)
                qk_high(14 + f, qmB[:, 0, f, :], 1)

            def pair_event(jj, s):
                n = N_ATB + 3 * jj + s
                ring(n + 2)
                if s < 2:
                    if jj:
                        act.wait_ge(sc_done, 2 * jj)
                    qk_high(16 + 2 * jj + s, qkB[:, s, 0, :], 1)

            def pair_v(jj):
                if jj >= 3:
                    act.wait_ge(bav, (4, 6, 8)[jj - 3])
                v_high(10 + jj, vB[:, jj % 3, 0, :, :], TR[:].rearrange("p (k f) -> p k f", k=TT))

            for g in range(6):
                mem_slot(1, g)
                for n in finished(MEM_FILL_B[g], N_ATB):
                    pair_event(0, n - N_ATB)
            pair_v(0)

            def scores(jj):
                g = jj % 3
                for hp in range(2):
                    act.wait_ge(bmax, 2 * jj + hp + 1)
                    for i, (o, w) in enumerate(score_blocks(g, hp)):
                        a, b = (own0[:, 0, hp], own0[:, 1, hp]) if g == 0 else (nmax[:, g, hp], den[:, g, hp])
                        nc.scalar.activation(scB[:, o:o + w], scB[:, o:o + w], ACT.Exp, bias=a[:, i:i + 1],
                                             accum_out=b[:, i:i + 1]).then_inc(bexp, 1)

            def ratios(jp):
                act.wait_ge(co_diff, jp + 1)
                nc.scalar.activation(st[:, 88:112], st[:, 88:112], ACT.Exp).then_inc(co_exp, 1)

            def batch_high(jp, b):
                n = P * len(BATCHES[b][2])
                c = 8 * jp + b
                act.wait_ge(bt_done, c + 1)
                if c >= 2:
                    act.wait_ge(bav, c if jp and b == 7 else c - 1)
                nc.scalar.activation(pT[pt_buffer(jp, b)][0][:, 0:n], banks[2 + b % 4][:, 0:n], ACT.Copy).then_inc(pt_hi, 1)

            def output_high(jp, b):
                if BATCHES[b][3]:
                    hi, lo, src, hd = out_views(jp, b)
                    act.wait_ge(bav, 8 * jp + b + 1)
                    nc.scalar.activation(hi, src, ACT.Copy).then_inc(o_hi, 1)

            for op, *a in SEQ_B:
                if op not in "OR":
                    {"S": scores, "P": pair_event, "V": pair_v, "G": ratios, "T": batch_high, "A": output_high}[op](*a)
            for k in range(KT):
                ring(N_OUTB + k + 2)
                absorb(3, k)
            ffn(1, N_UPB, N_DNB)
            for k in range(KT):
                act.wait_ge(h_ready, 32 + k + 1)
                if k >= 2:
                    act.wait_ge(fin_sq, k - 1)
                nc.scalar.activation(sq[:, k % 2, :], hT[:, k, :], ACT.Square).then_inc(sq_done, 1)
                act.wait_ge(sq_done, 32 + k + 1)
                nc.scalar.activation(hT[:, k, :], hT[:, k, :], ACT.Copy, scale=gain(G_FIN, k)).then_inc(fin_g, 1)
            act.wait_ge(fin_sq, KT)
            link(nc.scalar.activation(fin_t, fin_ss, ACT.Ln, scale=-1.0 / D, bias=st[:, 200:201]))
            nc.scalar.activation(fin_r, fin_t, ACT.Exp, scale=-0.5).then_inc(fin_guess, 1)
            act.wait_ge(fin_ready, 1)
            for q in range(2 * TT):
                if q not in FIN_DVE:
                    act.wait_ge(fin_tr, q + 1)
                    nc.scalar.activation(x_nat[:, q % TT, T * (q // TT):T * (q // TT + 1)], banks[FIN_BANK[q]][:],
                                         ACT.Copy, scale=fin_r[:, q % TT:q % TT + 1]).then_inc(fin_ev_act, 1)

        @block.vector
        def _(dve):
            def link(ins):
                selfcount["dve"] += 1
                ins.then_inc(dve_self, 1)
                dve.wait_ge(dve_self, selfcount["dve"])

            def ring(n, m=None):
                m = n if m is None else m
                dve.wait_ge(hi_done, n + 1)
                nc.vector.tensor_tensor(w_lo[:, m % SPLIT, :], raw[:, m % RAW, :], w_hi[:, m % SPLIT, :].bitcast(F32),
                                        ALU.subtract).then_inc(lo_done, 1)

            def absorb_low(e, k):
                g = (G_A, G_FA, G_B, G_FB)[e]
                dve.wait_ge(yhi, y_wait(e, k))
                nc.vector.scalar_tensor_tensor(out=y_lo[:, k, :], in0=hT[:, k, :], scalar=gain(g, k),
                                               in1=y_hi[:, k, :].bitcast(F32), op0=ALU.mult,
                                               op1=ALU.subtract).then_inc(ylo, 1)

            def rms(e):
                dve.wait_ge(r_guess, e + 1)
                link(nc.vector.tensor_tensor(sqn, rT[:], rT[:], ALU.mult))
                link(nc.vector.tensor_scalar(newt, TR[:], -1.0 / D, EPS, ALU.mult, ALU.add))
                link(nc.vector.tensor_tensor(sqn, sqn, newt, ALU.mult))
                link(nc.vector.tensor_scalar(sqn, sqn, -0.5, 1.5, ALU.mult, ALU.add))
                ins = nc.vector.tensor_tensor(rT[:], rT[:], sqn, ALU.mult)
                ins.then_inc(r_ready, 1)
                dve.wait_ge(r_ready, e + 1)

            def v_low(iv, dst, hi, src):
                dve.wait_ge(v_hi, iv + 1)
                nc.vector.tensor_tensor(dst, src, hi.bitcast(F32), ALU.subtract).then_inc(v_lo, 1)

            nc.vector.memset(st[:, 200:201], EPS).then_inc(dve_self, 1)
            selfcount["dve"] += 1
            dve.wait_ge(m_sq, 2)
            link(nc.vector.tensor_scalar(st[:, 4:6], st[:, 0:2], 1.0 / D, EPS, ALU.mult, ALU.add))
            nc.vector.memset(st[:, 201:202], 0.0).then_inc(m_var, 1)
            dve.wait_ge(m_exp, 1)
            link(nc.vector.tensor_tensor(st[:, 0:2], st[:, 6:8], st[:, 6:8], ALU.mult))
            link(nc.vector.tensor_tensor(st[:, 0:2], st[:, 0:2], st[:, 4:6], ALU.mult))
            link(nc.vector.tensor_scalar(st[:, 0:2], st[:, 0:2], -0.5, 1.5, ALU.mult, ALU.add))
            link(nc.vector.tensor_tensor(st[:, 6:8], st[:, 6:8], st[:, 0:2], ALU.mult))
            for t in range(2):
                nc.vector.tensor_scalar(m_nat[:, t, :], m_nat[:, t, :], st[:, 6 + t:7 + t], None,
                                        ALU.mult).then_inc(m_norm, 1)
            dve.wait_ge(tab_ready, 1)
            ring(0)
            for k in range(KT):
                for l, g in ((0, G_MA), (1, G_MB)):
                    dve.wait_ge(ym_hi, 2 * k + l + 1)
                    if l == 0:
                        dve.wait_ge(ym_hi, 2 * k + 2)
                    nc.vector.scalar_tensor_tensor(out=ym[:, l, 1, k, :], in0=YM_BANK[k % 3][:, 0:M],
                                                   scalar=gain(g, k), in1=ym[:, l, 0, k, :].bitcast(F32),
                                                   op0=ALU.mult, op1=ALU.subtract).then_inc(ym_lo, 1)
                if k == 1:
                    ring(1)

            def mem_v_low(iv):
                l, f = divmod(iv, 2)
                v_low(iv, vm[l][:, 1, :, P * f:P * (f + 1)], vm[l][:, 0, :, P * f:P * (f + 1)],
                      TR[:, 0:M].rearrange("p (k f) -> p k f", k=2))

            def x_tile(n):
                dve.wait_ge(x_tr, n + 1)
                nc.vector.tensor_copy(hT[:, n, :], banks[4 + n % 2][:]).then_inc(h_ready, 1)

            def mem_tile(n):
                l, f = divmod(n, 4)
                if f >= 2:
                    dve.wait_ge(tile_done, n + 1)
                    if f == 3 or l == 1:
                        dve.wait_ge(vt_tr, 2 * l + f - 2)
                    nc.vector.tensor_copy(m_vT, banks[n % 2][:, 0:M]).then_inc(evicted, 1)
                else:
                    dve.wait_ge(km_hi, 2 * l + f + 1)
                    nc.vector.tensor_tensor(km[l][:, 1, f, :], banks[n % 2][:, 0:M], km[l][:, 0, f, :].bitcast(F32),
                                            ALU.subtract).then_inc(evicted, 1)

            for n in range(8):
                if n:
                    x_tile(n)
                ring(n + 2)
                mem_tile(n)
                if n in (3, 4, 7):
                    mem_v_low(mem_value(n - 1))
                if n == 0:
                    dve.wait_ge(m_tr, KT)
                    x_tile(0)
                absorb_low(0, n)

            def qk_float(i, n, scale, l=0, residues=False):
                dve.wait_ge(tile_done, n + 1)
                if i:
                    dve.wait_ge(kq_lo, i)
                nc.vector.scalar_tensor_tensor(out=by_tile(qkfs[l]), in0=tokens(banks[n % 2][:], residues), scalar=scale,
                                               in1=tokens(rT[:], residues), op0=ALU.mult,
                                               op1=ALU.mult).then_inc(evicted, 1)
                dve.wait_ge(evicted, ev_count(n))
                nc.vector.engine_nop().then_inc(kq_f, 1)

            def qk_low(i, dst, hi, l=0):
                dve.wait_ge(kq_hi, i + 1)
                nc.vector.tensor_tensor(dst, qkfs[l], hi.bitcast(F32), ALU.subtract).then_inc(kq_lo, 1)

            def v_float(iv, n, l=0, residues=False):
                dve.wait_ge(tile_done, n + 1)
                dve.wait_ge(vt_tr, iv)
                nc.vector.tensor_tensor(by_tile(vTs[l]), tokens(banks[n % 2][:], residues), tokens(rT[:], residues),
                                        ALU.mult).then_inc(evicted, 1)

            def mem_slot(l, g):
                if g >= 2:
                    i = MH * l + g - 2
                    m = i % MH
                    r = DH * (m % 2)
                    dve.wait_ge(mo_hi, i + 1)
                    nc.vector.tensor_tensor(oT_lo[r:r + DH, 6 + m // 2, :], OB[0:DH, :],
                                            oT_hi[r:r + DH, 6 + m // 2, :].bitcast(F32), ALU.subtract).then_inc(mo_ev, 1)
                if 1 <= g <= MH:
                    i = MH * l + g - 1
                    for kt in range(2):
                        dve.wait_ge(mpt_hi, 2 * i + kt + 1)
                        nc.vector.tensor_tensor(pmTs[l][:, 1, kt, :], banks[4 + kt][:], pmTs[l][:, 0, kt, :].bitcast(F32),
                                                ALU.subtract).then_inc(mpt_lo, 1)
                if g < MH:
                    i = MH * l + g
                    dve.wait_ge(ms_done, i + 1)
                    for b in range(2):
                        ins = nc.vector.tensor_reduce(st[:, 8 + 2 * b:10 + 2 * b], banks[2 + b][:].rearrange("p (q k) -> p q k", q=2),
                                                      AX_X, ALU.max, negate=True)
                    ins.then_inc(mmx, 1)
                    dve.wait_ge(mexp, 4 * (i + 1))
                    link(nc.vector.reciprocal(st[:, 16:20], st[:, 12:16]))
                    for qt in range(TT):
                        ins = nc.vector.tensor_scalar(pm[:, M * qt:M * (qt + 1)], pm[:, M * qt:M * (qt + 1)],
                                                      st[:, 16 + qt:17 + qt], None, ALU.mult)
                    ins.then_inc(mpn, 1)

            def pair_v_low(j):
                v_low(4 + j, vv[:, j % 2, 1, :, :], vv[:, j % 2, 0, :, :], TR[:].rearrange("p (k f) -> p k f", k=TT))

            def fill_events(fill):
                for n in finished(fill):
                    j, s = divmod(n - N_ATA, 3)
                    if s < 2:
                        qk_float(2 + 2 * j + s, n, (QSCALE, 1.0)[s])
                    else:
                        v_float(4 + j, n)
                    ring(n + 2)
                    if s < 2:
                        qk_low(2 + 2 * j + s, qk[:, j % 2, s, 1, :], qk[:, j % 2, s, 0, :])

            ring(N_QMA + 2)
            mem_v_low(3)
            rms(0)
            qk_float(0, N_QMA, QSCALE)
            qk_low(0, qm[:, 1, 0, :], qm[:, 0, 0, :])
            qk_float(1, N_QMA + 1, QSCALE)
            ring(N_QMA + 3)
            qk_low(1, qm[:, 1, 1, :], qm[:, 0, 1, :])
            for g in range(6):
                mem_slot(0, g)
                for j in v_due(MEM_FILL, g):
                    pair_v_low(j)
                fill_events(MEM_FILL[g])
            for t in range(U + 5):
                if t >= 8 and t % 4 == 0:
                    hd = (t - 8) // 4
                    r = DH * (hd % 2)
                    dve.wait_ge(o_hi, hd + 1)
                    nc.vector.tensor_tensor(oT_lo[r:r + DH, hd // 2, :], OB[0:DH, :],
                                            oT_hi[r:r + DH, hd // 2, :].bitcast(F32), ALU.subtract).then_inc(o_ev, 1)
                if t < U:
                    n = unit(t)[3]
                    dve.wait_ge(z_done, t + 1)
                    if t >= 2:
                        dve.wait_ge(sp_max, t - 1)
                    nc.vector.tensor_scalar(ze[:, t % 2, 0:n], banks[2 + t % 4][:, 0:n], 30.0, None,
                                            ALU.min).then_inc(z_min, 1)
                if 1 <= t <= U:
                    u = t - 1
                    n = unit(u)[3]
                    dve.wait_ge(ln_done, u + 1)
                    if u >= 2:
                        dve.wait_ge(sp_lo, u - 1)
                    nc.vector.tensor_tensor(spf[:, u % 2, 0:n], banks[2 + u % 4][:, 0:n], ze[:, u % 2, 0:n],
                                            ALU.max).then_inc(sp_max, 1)
                for j in v_due(ATT_FILL, t):
                    pair_v_low(j)
                fill_events(ATT_FILL[t])
                if 3 <= t < U + 3:
                    u = t - 3
                    n = unit(u)[3]
                    dve.wait_ge(wt_hi, u + 1)
                    nc.vector.tensor_tensor(ww[:, u % 2, 1, 0:n], wf[:, u % 2, 0:n], ww[:, u % 2, 0, 0:n].bitcast(F32),
                                            ALU.subtract).then_inc(wt_lo, 1)
                if 1 <= t <= U:
                    u = t - 1
                    a, n = unit(u)[2:]
                    hd = u // 4
                    dve.wait_ge(sp_hi, u + 1)
                    o = slice(SPO[a], SPO[a] + n)
                    nc.vector.tensor_tensor(spb[:, hd % 2, 1, o], spf[:, u % 2, 0:n], spb[:, hd % 2, 0, o].bitcast(F32),
                                            ALU.subtract).then_inc(sp_lo, 1)

            def out_proj(e, n0):
                for k in range(KT):
                    n = n0 + k
                    dve.wait_ge(tile_done, n + 1)
                    link(nc.vector.tensor_tensor(hT[:, k, :], hT[:, k, :], banks[n % 2][:], ALU.add))
                    nc.vector.engine_nop().then_inc(h_ready, 1)
                    nc.vector.engine_nop().then_inc(evicted, 1)
                    ring(n + 2)
                    absorb_low(e, k)

            def ffn(l, n_up, n_dn):
                def tile(c, n, m, taps):
                    dve.wait_ge(tile_done, n + 1)
                    if m >= N_UPA + 2:
                        dve.wait_ge(tap_done, c - 1)
                    u, o = ub[:, m % 2, :], cb[:, m % 2, :]
                    nc.vector.tensor_tensor(u, banks[m % 2][:], rT[:], ALU.mult).then_inc(evicted, 1)
                    ring(n + 2, m + 2)
                    dve.wait_ge(tap_done, c + 1)
                    nc.vector.scalar_tensor_tensor(out=o[:, 1:T], in0=u[:, 0:T - 1], scalar=taps[1], in1=o[:, 1:T],
                                                   op0=ALU.mult, op1=ALU.add).then_inc(conv_half, 1)
                    dve.wait_ge(conv_half, c + 1)
                    nc.vector.scalar_tensor_tensor(out=o[:, 2:T], in0=u[:, 0:T - 2], scalar=taps[0], in1=o[:, 2:T],
                                                   op0=ALU.mult, op1=ALU.add).then_inc(conv_done, 1)

                def pair(q, n, m, col):
                    tile(q * 2, n, m, [col(t, 0) for t in range(2)])
                    tile(q * 2 + 1, n + 1, m + 1, [col(t, 1) for t in range(2)])
                    dve.wait_ge(conv_done, q * 2 + 2)
                    dve.wait_ge(silu_done, q + 1)
                    nc.vector.tensor_tensor(prod, cb[:, 0, :], sg, ALU.mult).then_inc(prod_done, 1)
                    dve.wait_ge(act_hi_done, q + 1)
                    k = slice(q - FT * l, q - FT * l + 1) if isinstance(q, int) else bass.ds(q - FT * l, 1)
                    nc.vector.tensor_tensor(act_lo[:, k, :], prod, act_hi[:, k, :].bitcast(F32),
                                            ALU.subtract).then_inc(act_lo_done, 1)

                base = 3 * l * 2 * FT
                rms(2 * l + 1)
                pair(FT * l, n_up, n_up, lambda t, s: conv[:, base + (2 * t + s) * FT:base + (2 * t + s) * FT + 1])
                with dve.Fori(0, 7) as i:
                    for j in range(3):
                        pair(i * 3 + (FT * l + 1 + j), i * 6 + (n_up + 2 + 2 * j), n_up + 2 + 2 * j,
                             lambda t, s: conv[:, bass.ds(i * 3 + (base + (2 * t + s) * FT + 1 + j), 1)])
                ring(n_dn + 2)
                ring(n_dn + 3)
                with dve.Fori(0, 3) as i:
                    for j in range(6):
                        ring(i * 6 + (n_dn + 4 + j), n_dn + 4 + j)
                if l == 0:
                    ring(N_QMB)
                for k in range(KT):
                    if k < KT - 1:
                        dve.wait_ge(down_done, 7 * (FT * (l + 1) - 1) + k + 1)
                    else:
                        dve.wait_ge(tile_done, n_dn + FT)
                    nc.vector.tensor_tensor(hT[:, k, :], hT[:, k, :], banks[k][:], ALU.add).then_inc(h_ready, 1)
                    if l == 0:
                        if k:
                            absorb_low(2, k - 1)
                        if k == 4:
                            ring(N_QMB + 1)
                        dve.wait_ge(h_ready, 16 + k + 1)
                if l == 0:
                    absorb_low(2, KT - 1)

            out_proj(1, N_OUTA)
            ffn(0, N_UPA, N_DNA)

            def shared_low(ks):
                for k in ks:
                    dve.wait_ge(yhi, ykv_wait(k))
                    nc.vector.scalar_tensor_tensor(out=ykv_lo[:, k, :], in0=hT[:, k, :], scalar=gain(G_KV, k),
                                                   in1=ykv_hi[:, k, :].bitcast(F32), op0=ALU.mult,
                                                   op1=ALU.subtract).then_inc(ylo, 1)

            shared_low(range(4))
            rms(2)
            for f in range(2):
                if f:
                    shared_low(range(4, KT))
                qk_float(14 + f, N_QMB + f, QSCALE, 1)
                ring(N_QMB + f + 2)
                qk_low(14 + f, qmB[:, 1, f, :], qmB[:, 0, f, :], 1)

            def pair_event(jj, s):
                n = N_ATB + 3 * jj + s
                g = jj % 3
                if s < 2:
                    qk_float(16 + 2 * jj + s, n, (1.0, QSCALE)[s], 1, g > 0)
                else:
                    v_float(10 + jj, n, 1, g > 0)
                ring(n + 2)
                if s < 2:
                    qk_low(16 + 2 * jj + s, qkB[:, s, 1, :], qkB[:, s, 0, :], 1)

            def pair_v(jj):
                v_low(10 + jj, vB[:, jj % 3, 1, :, :], vB[:, jj % 3, 0, :, :], TR[:].rearrange("p (k f) -> p k f", k=TT))

            for g in range(6):
                mem_slot(1, g)
                for n in finished(MEM_FILL_B[g], N_ATB):
                    pair_event(0, n - N_ATB)
            pair_v(0)

            def scores(jj):
                jp, g = divmod(jj, 3)
                for hp in range(2):
                    h = 2 * B_ORDER[jj] + hp
                    dve.wait_ge(sc_done, 2 * jj + hp + 1)
                    if jp:
                        dve.wait_ge(bt_done, (4, 6, 8)[g])
                        dve.wait_ge(co_gather, jp)
                        dve.wait_ge(co_exp, jp)
                    width = 2 * P if g == 0 else P
                    c = (C_D0, C_D1, C_D2)[g] - CS_FROM
                    link(nc.vector.tensor_scalar(biasB[:, 0:width], cs[:, c:c + width], slope(h), None, ALU.mult))
                    for i, (o, w) in enumerate(score_blocks(g, hp)):
                        link(nc.vector.tensor_tensor_reduce(
                            out=scB[:, o:o + w], in0=score_bank(g, hp, i, w), in1=biasB[:, width - w:width], scale=1.0,
                            scalar=-3e38, op0=ALU.add, op1=ALU.max, accum_out=smax[:, i:i + 1]))
                    dst = own0[:, 0, hp, :] if g == 0 else nmax[:, g, hp, :]
                    nc.vector.tensor_scalar(dst, smax, -1.0, None, ALU.mult).then_inc(bmax, 1)
                    dve.wait_ge(bmax, 2 * jj + hp + 1)

            def coefficients(jp):
                dve.wait_ge(bexp, 24 * (jp + 1))
                dve.wait_ge(co_gather, jp + 1)
                for x, dst in ((0, nmax), (1, den)):
                    link(nc.vector.tensor_copy(dst[:, 0, :, :], TR[:, 0:16].rearrange("p (r x h) -> p x h r", r=4, x=2)[:, x]))
                link(nc.vector.tensor_tensor(nmin, nmax[:, 0], nmax[:, 1], ALU.min))
                link(nc.vector.tensor_tensor(nmin, nmin, nmax[:, 2], ALU.min))
                for g in range(3):
                    ins = nc.vector.tensor_tensor(coef[:, g], nmin, nmax[:, g], ALU.subtract)
                ins.then_inc(co_diff, 1)
                dve.wait_ge(co_exp, jp + 1)
                link(nc.vector.tensor_tensor(den, den, coef, ALU.mult))
                link(nc.vector.tensor_tensor(total, den[:, 0], den[:, 1], ALU.add))
                link(nc.vector.tensor_tensor(total, total, den[:, 2], ALU.add))
                link(nc.vector.reciprocal(total, total))
                for g in range(3):
                    link(nc.vector.tensor_tensor(coef[:, g], coef[:, g], total, ALU.mult))
                link(nc.vector.memset(st[:, 128:160], 0.0))
                for i in range(4):
                    a = slice(32 * i, 32 * (i + 1))
                    ins = nc.vector.tensor_copy(coef0x[a, i], coef[a, 0])
                ins.then_inc(co_spread, 1)

            def scale_weights(jp):
                dve.wait_ge(co_back, jp + 1)
                link(nc.vector.tensor_copy(coef0, TR[:, 32:40].rearrange("p (i h) -> p i h", i=4)))
                for g in range(3):
                    for hp in range(2):
                        for i, (o, w) in enumerate(score_blocks(g, hp)):
                            c = coef0[:, i, hp:hp + 1] if g == 0 else coef[:, g, hp, i:i + 1]
                            nc.vector.tensor_scalar(scB[:, o:o + w], scB[:, o:o + w], c, None, ALU.mult).then_inc(scaled, 1)

            def batch_low(jp, b):
                n = P * len(BATCHES[b][2])
                buf = pT[pt_buffer(jp, b)]
                dve.wait_ge(pt_hi, 8 * jp + b + 1)
                nc.vector.tensor_tensor(buf[1][:, 0:n], banks[2 + b % 4][:, 0:n], buf[0][:, 0:n].bitcast(F32),
                                        ALU.subtract).then_inc(pt_lo, 1)

            def output_low(jp, b):
                if BATCHES[b][3]:
                    hi, lo, src, hd = out_views(jp, b)
                    dve.wait_ge(o_hi, 12 + hd + 1)
                    nc.vector.tensor_tensor(lo, src, hi.bitcast(F32), ALU.subtract).then_inc(o_ev, 1)

            for op, *a in SEQ_B:
                if op != "O":
                    {"S": scores, "P": pair_event, "V": pair_v, "G": coefficients, "R": scale_weights,
                     "T": batch_low, "A": output_low}[op](*a)
            out_proj(3, N_OUTB)
            ffn(1, N_UPB, N_DNB)
            dve.wait_ge(fin_guess, 1)
            link(nc.vector.tensor_scalar(fin_v, fin_ss, -1.0 / D, EPS, ALU.mult, ALU.add))
            link(nc.vector.tensor_tensor(fin_t, fin_r, fin_r, ALU.mult))
            link(nc.vector.tensor_tensor(fin_t, fin_t, fin_v, ALU.mult))
            link(nc.vector.tensor_scalar(fin_t, fin_t, -0.5, 1.5, ALU.mult, ALU.add))
            nc.vector.tensor_tensor(fin_r, fin_r, fin_t, ALU.mult).then_inc(fin_ready, 1)
            dve.wait_ge(fin_ready, 1)
            for q in FIN_DVE:
                dve.wait_ge(fin_tr, q + 1)
                nc.vector.tensor_scalar(x_nat[:, q % TT, T * (q // TT):T * (q // TT + 1)], banks[FIN_BANK[q]][:],
                                        fin_r[:, q % TT:q % TT + 1], None, ALU.mult).then_inc(fin_ev_dve, 1)

        @block.tensor
        def _(pe):
            mm = nc.tensor.matmul

            def steps(n, m, ks, y, y_ready=None, width=T):
                bank = banks[m % 2][:, 0:width]
                for k in ks:
                    if y_ready is not None:
                        y_ready(k)
                    w = [t[:, m % SPLIT, P * k:P * (k + 1)] for t in (w_hi, w_lo)]
                    mm(bank, w[0], y[0][:, k, :], start=(k == 0), stop=False)
                    mm(bank, w[0], y[1][:, k, :], start=False, stop=False)
                    last = mm(bank, w[1], y[0][:, k, :], start=False, stop=(k == KT - 1))
                if KT - 1 in ks:
                    last.then_inc(tile_done, 1)

            def tile(n, m, l, y, y_ready=None, width=T):
                pe.wait_ge(lo_done, n + 1)
                if m >= 2:
                    pe.wait_ge(evicted, n - 1 - 22 * l)
                steps(n, m, range(KT), y, y_ready, width)

            def sum_squares(e):
                pe.wait_ge(ss_add, 8 * (e + 1))
                if e:
                    pe.wait_ge(r_ready, e)
                pe.wait_ge(v_lo, (4, 10, 10, 16)[e])
                mm(TR[:], nones, ss[:], start=True, stop=True).then_inc(ss_done, 1)

            pe.wait_ge(ld_cst, 32)
            pe.wait_ge(ld_g, 16 * 8)
            pe.wait_ge(ld_cw, 32)
            nc.tensor.transpose(TR[:, 0:64], gv[0:64, :], ident[0:64, 0:64])
            for l, nat in enumerate((cw_nat, cw2_nat)):
                for t in range(3):
                    o = 64 + (3 * l + t) * 2 * FT
                    last = nc.tensor.transpose(TR[:, o:o + 2 * FT], nat[0:2 * FT, P * t:P * (t + 1)],
                                               ident[0:2 * FT, 0:2 * FT])
            last.then_inc(tab_tr, 1)
            pe.wait_ge(m_norm, 2)
            for k in range(KT):
                if k >= 3:
                    pe.wait_ge(ym_lo, 2 * (k - 2))
                for t in range(2):
                    last = nc.tensor.transpose(YM_BANK[k % 3][:, P * t:P * (t + 1)], m_nat[:, t, P * k:P * (k + 1)], ident)
                last.then_inc(m_tr, 1)

            def v_transpose(iv, count):
                pe.wait_ge(vt_ready_of(iv)[0], vt_ready_of(iv)[1])
                src = m_vT if count == 2 else vTs[iv >= 10]
                if iv:
                    pe.wait_ge(v_lo, iv)
                for t in range(count):
                    last = nc.tensor.transpose(TR[:, P * t:P * (t + 1)], src[:, P * t:P * (t + 1)], ident)
                last.then_inc(vt_tr, 1)

            def vt_ready_of(iv):
                n = (2, 3, 6, 7)[iv] if iv < 4 else (N_ATA if iv < 10 else N_ATB) + 3 * ((iv - 4) % 6) + 2
                return evicted, ev_count(n)

            pe.wait_ge(tab_ready, 1)
            def x_transposes(n):
                pe.wait_ge(ld_x, 16)
                if n >= 2:
                    pe.wait_ge(h_ready, n - 1)
                for t in range(TT):
                    last = nc.tensor.transpose(banks[4 + n % 2][:, P * t:P * (t + 1)], x_nat[:, t, P * n:P * (n + 1)], ident)
                last.then_inc(x_tr, 1)

            for n in range(8):
                if n:
                    x_transposes(n)

                def ready(k):
                    if n == 0:
                        pe.wait_ge(ym_lo, 2 * k + 2)
                l = n // 4
                tile(n, n, 0, (ym[:, l, 0], ym[:, l, 1]), ready, M)
                if n in (3, 4, 7):
                    v_transpose(mem_value(n - 1), 2)
                if n == 0:
                    x_transposes(0)

            y = (y_hi, y_lo)
            tile(N_QMA, N_QMA, 0, y, lambda k: pe.wait_ge(ylo, y_wait(0, k)))
            v_transpose(3, 2)
            sum_squares(0)
            tile(N_QMA + 1, N_QMA + 1, 0, y)

            def mem_scores(i, km, last_q):
                m = i % MH
                r, f = DH * (m % 2), m // 2
                pe.wait_ge(kq_lo, last_q)
                if i:
                    pe.wait_ge(mexp, 4 * i)
                for qt in range(TT):
                    o = banks[2 + qt // 2][:, M * (qt % 2):M * (qt % 2) + M]
                    for s, (a, b) in enumerate(((0, 0), (0, 1), (1, 0))):
                        last = mm(o, qms[i // MH][r:r + DH, a, f, P * qt:P * (qt + 1)], km[r:r + DH, b, f, :],
                                  start=(s == 0), stop=(s == 2))
                last.then_inc(ms_done, 1)

            def mem_transposes(i):
                pe.wait_ge(mpn, i + 1)
                if i:
                    pe.wait_ge(mpt_lo, 2 * i)
                for kt in range(2):
                    for qt in range(TT):
                        last = nc.tensor.transpose(banks[4 + kt][:, P * qt:P * (qt + 1)],
                                                   pm[:, M * qt + P * kt:M * qt + P * (kt + 1)], ident)
                last.then_inc(mt_done, 1)

            def mem_values(i, vm):
                m = i % MH
                if i:
                    pe.wait_ge(mo_ev, i)
                for kt in range(2):
                    pe.wait_ge(mpt_lo, 2 * i + kt + 1)
                    for s, (a, b) in enumerate(((0, 0), (0, 1), (1, 0))):
                        last = mm(OB[0:DH, :], vm[:, a, kt, DH * m:DH * (m + 1)], pmTs[i // MH][:, b, kt, :],
                                  start=(kt == 0 and s == 0), stop=(kt == 1 and s == 2))
                last.then_inc(mav, 1)

            def mem_slot(l, g, last_q):
                if g >= 2:
                    mem_values(MH * l + g - 2, vm[l])
                if 1 <= g <= MH:
                    mem_transposes(MH * l + g - 1)
                if g < MH:
                    mem_scores(MH * l + g, km[l], last_q)

            def fill(span):
                if not span:
                    return
                s = span[0]
                while s < span[1]:
                    n, k = N_ATA + s // 8, s % 8
                    e = min(span[1], s - k + 8)
                    if k == 0:
                        pe.wait_ge(lo_done, n + 1)
                        pe.wait_ge(evicted, n - 1)
                    steps(n, n, range(k, k + e - s), y)
                    s = e

            def out_step(l, n, k):
                ks = OUT_KS[l]
                if k == ks[0]:
                    pe.wait_ge(lo_done, n + 1)
                    pe.wait_ge(evicted, n - 1 - 22 * l)
                if k < PAIRS:
                    pe.wait_ge(o_ev, 2 * PAIRS * l + 2 * (ks.index(k) - 1))
                else:
                    pe.wait_ge(mo_ev, MH * (l + 1))
                w = [t[:, n % SPLIT, P * k:P * (k + 1)] for t in (w_hi, w_lo)]
                mm(banks[n % 2][:], w[0], oT_hi[:, k, :], start=(k == ks[0]), stop=False)
                mm(banks[n % 2][:], w[0], oT_lo[:, k, :], start=False, stop=False)
                last = mm(banks[n % 2][:], w[1], oT_hi[:, k, :], start=False, stop=(k == ks[-1]))
                if k == ks[-1]:
                    last.then_inc(tile_done, 1)

            def out_proj(l, n0, done):
                for x in range(KT):
                    for k in OUT_KS[l]:
                        if (n0 + x, k) not in done:
                            out_step(l, n0 + x, k)

            for g in range(6):
                mem_slot(0, g, 2)
                for j in v_due(MEM_FILL, g):
                    v_transpose(4 + j, TT)
                fill(MEM_FILL[g])

            for t in range(U + 5):
                if t < U:
                    j, hp, a, n = unit(t)
                    r = DH * hp
                    o = banks[2 + t % 4][:, 0:n]
                    if t >= 4:
                        pe.wait_ge(w_exp, t - 3)
                    else:
                        pe.wait_ge(mexp, 4 * MH)
                        pe.wait_ge(mpt_lo, 2 * MH)
                    if t % 8 == 0:
                        pe.wait_ge(kq_lo, 2 + 2 * j + 2)
                    for s, (b, c) in enumerate(((0, 0), (0, 1), (1, 0))):
                        mm(o, qk[r:r + DH, j % 2, 1, b, P * a:P * (a + 1)], qk[r:r + DH, j % 2, 0, c, P * a:T],
                           start=(s == 0), stop=False, skip_group_check=True)
                    mm(o[:, 0:P], ident_r, mask_r, start=False, stop=True, skip_group_check=True).then_inc(z_done, 1)
                for j in v_due(ATT_FILL, t):
                    v_transpose(4 + j, TT)
                fill(ATT_FILL[t])
                for n, k in OUT_SLOT.get(t, ()):
                    out_step(0, n, k)
                if 4 <= t < U + 4:
                    u = t - 4
                    j, hp, a, n = unit(u)
                    hd = u // 4
                    pe.wait_ge(wt_lo, u + 1)
                    if a == 3 and hd:
                        pe.wait_ge(o_ev, hd)
                    if u % 8 == 0:
                        pe.wait_ge(v_lo, 4 + j + 1)
                    if u == 0:
                        pe.wait_ge(mo_ev, MH)
                    for s, (b, c) in enumerate(((0, 0), (0, 1), (1, 0))):
                        last = mm(OB[0:DH, P * a:T], vv[:, j % 2, b, a, DH * hp:DH * (hp + 1)], ww[:, u % 2, c, 0:n],
                                  start=(a == 3 and s == 0), stop=(a == 0 and s == 2), skip_group_check=True)
                    last.then_inc(av_done, 1)
                if 2 <= t < U + 2:
                    u = t - 2
                    a = unit(u)[2]
                    hd = u // 4
                    pe.wait_ge(sp_lo, u + 1)
                    for b in range(3, a - 1, -1):
                        nb = T - P * b
                        for s in range(2):
                            last = mm(banks[2 + u % 4][:, P * (b - a):P * (b - a) + nb], ntri_r if b == a else nones_r,
                                      spb[:, hd % 2, s, SPO[b]:SPO[b] + nb], start=False,
                                      stop=(b == a and s == 1), skip_group_check=True)
                    last.then_inc(cum_done, 1)

            def ffn(l, n_up, n_dn):
                e = 2 * l + 1
                tile(n_up, n_up, l, y, lambda k: pe.wait_ge(ylo, y_wait(e, k)))
                sum_squares(e)
                tile(n_up + 1, n_up + 1, l, y)
                with pe.Fori(0, 7) as i:
                    for j in range(6):
                        tile(i * 6 + (n_up + 2 + j), n_up + 2 + j, l, y)

                def down(k, n, m, first):
                    pe.wait_ge(lo_done, n + 1)
                    pe.wait_ge(act_lo_done, k + (FT * l + 1))
                    kk = slice(k, k + 1) if isinstance(k, int) else bass.ds(k, 1)
                    for f in range(KT):
                        w = [t[:, m % SPLIT, P * f:P * (f + 1)] for t in (w_hi, w_lo)]
                        for s, (a, b) in enumerate(((w[0], act_hi), (w[0], act_lo), (w[1], act_hi))):
                            last = mm(banks[f][:], a, b[:, kk, :], start=(first and s == 0), stop=(s == 2),
                                      skip_group_check=True)
                        last.then_inc(down_done if f < KT - 1 else tile_done, 1)

                pe.wait_ge(evicted, ev_count(n_dn - 1))
                for k in range(4):
                    down(k, n_dn + k, n_dn + k, k == 0)
                with pe.Fori(0, 3) as i:
                    for j in range(6):
                        down(i * 6 + (4 + j), i * 6 + (n_dn + 4 + j), n_dn + 4 + j, False)

            out_proj(0, N_OUTA, OUT_FILL)
            ffn(0, N_UPA, N_DNA)

            tile(N_QMB, N_QMB, 1, y, lambda k: pe.wait_ge(ylo, y_wait(2, k)))
            sum_squares(2)
            tile(N_QMB + 1, N_QMB + 1, 1, y)
            ykv = (ykv_hi, ykv_lo)

            def pair_steps(jj, s, ks=range(KT)):
                n = N_ATB + 3 * jj + s
                if jj == 0 and s == 0:
                    pe.wait_ge(ylo, ykv_wait(max(ks)))
                if 0 in ks:
                    pe.wait_ge(lo_done, n + 1)
                    pe.wait_ge(evicted, n - 1 - 22)
                steps(n, n, ks, (ykv, y, ykv)[s])

            pair_steps(0, 0, range(5))
            for g in range(6):
                mem_slot(1, g, 16)
                if MEM_FILL_B[g]:
                    a, b = MEM_FILL_B[g]
                    while a < b:
                        e = min(b, a - a % 8 + 8)
                        pair_steps(0, a // 8, range(a % 8, a % 8 + e - a))
                        a = e
            v_transpose(10, TT)

            def scores(jj):
                jp, g = divmod(jj, 3)
                pe.wait_ge(kq_lo, 16 + 2 * jj + 2)
                if jj:
                    pe.wait_ge(bmax, 2 * jj)
                else:
                    pe.wait_ge(mpt_lo, 4 * MH)
                if jp:
                    pe.wait_ge(pt_lo, (4, 6, 8)[g])
                for hp in range(2):
                    r = slice(DH * hp, DH * (hp + 1))
                    for i, (_, w) in enumerate(score_blocks(g, hp)):
                        c = P * (i + 1) - w
                        for s, (a, b) in enumerate(((0, 0), (0, 1), (1, 0))):
                            last = mm(score_bank(g, hp, i, w), qkB[r, 1, a, P * i:P * (i + 1)],
                                      qkB[r, 0, b, c:c + w], start=(s == 0), stop=(s == 2))
                    last.then_inc(sc_done, 1)

            def coefficients(jp):
                pe.wait_ge(bexp, 24 * (jp + 1))
                pe.wait_ge(v_lo, (13, 16)[jp])
                for i in range(4):
                    for r in range(4):
                        last = mm(TR[32 * i:32 * (i + 1), 4 * r:4 * r + 4], ident[:, r::4], own0[:, :, :, i],
                                  start=True, stop=True)
                last.then_inc(co_gather, 1)

            def coefficients_back(jp):
                pe.wait_ge(co_spread, jp + 1)
                for r in range(4):
                    c = C_E - CS_FROM + P * r
                    last = mm(TR[:, 32:40], cs[:, c:c + P], coef0x[:, :, :, r], start=(r == 0), stop=(r == 3))
                last.then_inc(co_back, 1)

            def batch_transposes(jp, b):
                blocks = BATCHES[b][2]
                pe.wait_ge(scaled, 24 * jp + sum(len(set(x[2] for x in t[2])) for t in BATCHES[:b + 1]))
                pe.wait_ge(bmax, 12 if jp else (6, 6, 6, 6, 8, 8, 10, 10)[b])
                if b >= 4:
                    pe.wait_ge(pt_lo, 8 * jp + b - 3)
                for x, (o, _, _, _, _) in enumerate(blocks):
                    last = nc.tensor.transpose(banks[2 + b % 4][:, P * x:P * (x + 1)], scB[:, o:o + P], ident)
                last.then_inc(bt_done, 1)

            def batch_values(jp, b):
                g, hp, blocks, _ = BATCHES[b]
                heads = sum(t[3] for t in BATCHES[:b])
                pe.wait_ge(pt_lo, 8 * jp + b + 1)
                pe.wait_ge(v_lo, 10 + 3 * jp + g + 1)
                pe.wait_ge(o_ev, 12 + 6 * jp + heads)
                if jp == 0:
                    pe.wait_ge(mo_ev, 2 * MH)
                buf = pT[pt_buffer(jp, b)]
                for x, (_, kb, i, first, final) in enumerate(blocks):
                    for s, (c, d) in enumerate(((0, 0), (0, 1), (1, 0))):
                        last = mm(OB[0:DH, P * i:P * (i + 1)], vB[:, g, c, kb, DH * hp:DH * (hp + 1)],
                                  buf[d][:, P * x:P * (x + 1)], start=(first and s == 0), stop=(final and s == 2))
                last.then_inc(bav, 1)

            for op, *a in SEQ_B:
                {"S": scores, "P": pair_steps, "V": lambda jj: v_transpose(10 + jj, TT), "G": coefficients,
                 "R": coefficients_back, "T": batch_transposes, "A": batch_values,
                 "O": lambda n, k: out_step(1, n, k)}[op](*a)
            out_proj(1, N_OUTB, OUT_B)
            ffn(1, N_UPB, N_DNB)
            def result_block(q):
                hf, t = divmod(q, TT)
                pe.wait_ge(fin_g, 4 * (hf + 1))
                pe.wait_ge(h_ready, 32 + max(4 * (hf + 1), FIN_BANK[q] + 1))
                if q == 7:
                    pe.wait_ge(fin_ev_act, 1)
                for x in range(4):
                    last = nc.tensor.transpose(banks[FIN_BANK[q]][:, P * x:P * (x + 1)],
                                               hT[:, 4 * hf + x, P * t:P * (t + 1)], ident)
                last.then_inc(fin_tr, 1)

            for k in range(KT):
                pe.wait_ge(sq_done, 32 + k + 1)
                for t in range(TT):
                    last = mm(fin_ss[:, t:t + 1], sq[:, k % 2, P * t:P * (t + 1)], nones[:, 0:1],
                              start=(k == 0 and t == 0), stop=(k == KT - 1), skip_group_check=True)
                last.then_inc(fin_sq, 1)
                if k == 5:
                    for q in range(TT):
                        result_block(q)
            for q in range(TT, 2 * TT):
                result_block(q)


_INS = ['x', 'mem', 'a_norm_attn', 'a_w_in', 'a_w_out', 'a_norm_mem', 'a_w_mem_kv', 'a_norm_ffn', 'a_ffn_up', 'a_ffn_conv',
        'a_ffn_down', 'kv_norm', 'w_kv_shared', 'b_norm_attn', 'b_w_in', 'b_w_out', 'b_norm_mem', 'b_w_mem_kv',
        'b_norm_ffn', 'b_ffn_up', 'b_ffn_conv', 'b_ffn_down', 'final_norm']


def kernel(**inputs):
    import concourse.bacc as bacc
    from concourse.bass_utils import run_bass_kernel_spmd

    nc = bacc.Bacc("TRN2", target_bir_lowering=False, num_devices=1)
    arrays, args = {}, []
    for name in _INS:
        arrays[f"in_{name}"] = np.ascontiguousarray(inputs[name])
    arrays["in_constants"] = constants()
    for name, a in arrays.items():
        args.append(nc.dram_tensor(name, a.shape, mybir.dt.from_np(a.dtype), kind="ExternalInput").ap())
    args.append(nc.dram_tensor("out", (1, T, D), F32, kind="ExternalOutput").ap())
    build(nc, *args)
    r = run_bass_kernel_spmd(nc, [arrays], core_ids=[0])
    return r.results[0]["out"]
```
